# Optimizing a Trainium2 kernel written in Bass

```python
import jax, jax.numpy as jnp
from jax import lax
import numpy as np

D_MODEL = 1024
BATCH = 1
SEQ = 512
DEPTH = 2

CHUNK = 64
N_EVEN = (DEPTH + 1) // 2
N_ODD = DEPTH // 2
D_MIX = D_MODEL
D_A = D_MIX // 2
A_HEADS = 8
A_HEAD_DIM = D_A // A_HEADS
A_CONV = 4
LRU_C = 8.0
D_B = D_MIX // 2
B_GROUPS = 8
B_GROUP_DIM = D_B // B_GROUPS
SGU_BLOCK = 128
N_HEADS = 16
HEAD_DIM = D_MODEL // N_HEADS
N_PREV_CHUNKS = 8
BAND = (N_PREV_CHUNKS + 1) * CHUNK
MAX_REL = 256
N_REL = 2 * MAX_REL + 1
D_FF = 2752
FFN_CONV = 3
EPS = 1e-6
NEG_INF = -1e30

kernel_name = "hybrid_rglru_sgu_bandattn_convffn"

def rms_norm(x, g):
    xf = x.astype(jnp.float32)
    y = xf * lax.rsqrt(jnp.mean(xf * xf, axis=-1, keepdims=True) + EPS)
    return (y * g.astype(jnp.float32)).astype(x.dtype)

def layer_norm(x, g, b):
    xf = x.astype(jnp.float32)
    mu = jnp.mean(xf, axis=-1, keepdims=True)
    xc = xf - mu
    var = jnp.mean(xc * xc, axis=-1, keepdims=True)
    y = xc * lax.rsqrt(var + EPS) * g.astype(jnp.float32) + b.astype(jnp.float32)
    return y.astype(x.dtype)

def causal_dwconv(x, w, b):
    k, c = w.shape
    y = lax.conv_general_dilated(
        x, w[:, None, :].astype(x.dtype), window_strides=(1,), padding=[(k - 1, 0)],
        dimension_numbers=('NWC', 'WIO', 'NWC'), feature_group_count=c)
    return y + b

def rg_lru(x, w_r, b_r, w_i, b_i, lam):
    bsz, s, _ = x.shape
    xh = x.reshape(bsz, s, A_HEADS, A_HEAD_DIM)
    r = jax.nn.sigmoid((jnp.einsum('bshi,hij->bshj', xh, w_r).reshape(bsz, s, D_A) + b_r).astype(jnp.float32))
    i = jax.nn.sigmoid((jnp.einsum('bshi,hij->bshj', xh, w_i).reshape(bsz, s, D_A) + b_i).astype(jnp.float32))
    log_a = -LRU_C * r * jax.nn.softplus(-lam.astype(jnp.float32))
    a = jnp.exp(log_a)
    u = jnp.sqrt(-jnp.expm1(2.0 * log_a)) * (i * x.astype(jnp.float32))

    def combine(left, right):
        a1, b1 = left
        a2, b2 = right
        return a1 * a2, a2 * b1 + b2

    _, h = lax.associative_scan(combine, (a, u), axis=1)
    return h.astype(x.dtype)

def spatial_gating(u, v, ln_g, ln_b, w_s, b_s):
    bsz, s, _ = v.shape
    v = layer_norm(v, ln_g, ln_b)
    nb = s // SGU_BLOCK
    vb = v.reshape(bsz, nb, SGU_BLOCK, B_GROUPS, B_GROUP_DIM)
    chunk_id = jnp.arange(SGU_BLOCK) // CHUNK
    mask = (chunk_id[:, None] >= chunk_id[None, :]).astype(w_s.dtype)
    w = w_s * mask[None]
    mixed = jnp.einsum('gij,bnjgc->bnigc', w, vb) + jnp.transpose(b_s)[None, None, :, :, None]
    return u * mixed.reshape(bsz, s, D_B)

def rglru_sgu_mixer(h, w_in, conv_w, conv_b, w_r, b_r, w_i, b_i, lam, ln_g, ln_b, w_s, b_s, w_out):
    z = h @ w_in
    a_x, a_g, b_u, b_v = jnp.split(z, 4, axis=-1)
    a_x = causal_dwconv(a_x, conv_w, conv_b)
    y_a = rg_lru(a_x, w_r, b_r, w_i, b_i, lam) * jax.nn.gelu(a_g)
    y_b = spatial_gating(jax.nn.gelu(b_u), jax.nn.gelu(b_v), ln_g, ln_b, w_s, b_s)
    return jnp.concatenate([y_a, y_b], axis=-1) @ w_out

def chunk_band_attention(h, w_qkv, rel_bias, w_o):
    bsz, s, _ = h.shape
    nc = s // CHUNK
    qkv = (h @ w_qkv).reshape(bsz, s, 3, N_HEADS, HEAD_DIM)
    q, k, v = qkv[:, :, 0], qkv[:, :, 1], qkv[:, :, 2]
    pad = N_PREV_CHUNKS * CHUNK
    kp = jnp.pad(k, ((0, 0), (pad, 0), (0, 0), (0, 0)))
    vp = jnp.pad(v, ((0, 0), (pad, 0), (0, 0), (0, 0)))
    qi = jnp.arange(CHUNK)
    ki = jnp.arange(BAND)
    rel = jnp.clip(pad + qi[:, None] - ki[None, :], -MAX_REL, MAX_REL) + MAX_REL
    bias = rel_bias[:, rel].astype(jnp.float32)
    scale = HEAD_DIM ** -0.5

    def one_chunk(c):
        start = c * CHUNK
        qc = lax.dynamic_slice_in_dim(q, start, CHUNK, axis=1)
        kc = lax.dynamic_slice_in_dim(kp, start, BAND, axis=1)
        vc = lax.dynamic_slice_in_dim(vp, start, BAND, axis=1)
        sc = jnp.einsum('bqhd,bkhd->bhqk', qc, kc).astype(jnp.float32) * scale + bias[None]
        valid = ki >= pad - start
        sc = jnp.where(valid[None, None, None, :], sc, NEG_INF)
        p = jax.nn.softmax(sc, axis=-1).astype(vc.dtype)
        return jnp.einsum('bhqk,bkhd->bqhd', p, vc)

    out = lax.map(one_chunk, jnp.arange(nc))
    out = jnp.moveaxis(out, 0, 1).reshape(bsz, s, D_MODEL)
    return out @ w_o

def conv_ffn(h, w_up, conv_w, conv_b, w_down):
    z = causal_dwconv(h @ w_up, conv_w, conv_b)
    g, u = jnp.split(z, 2, axis=-1)
    return (jax.nn.silu(g) * u) @ w_down

def setup_inputs(seed: int = 0) -> dict:
    key = jax.random.key(seed)
    ks = jax.random.split(key, 32)
    f32 = jnp.float32

    def nrm(k, shape, scale):
        return jax.random.normal(k, shape, f32) * scale

    def gain(k, shape):
        return 1.0 + 0.02 * jax.random.normal(k, shape, f32)

    x = jax.random.normal(ks[0], (BATCH, SEQ, D_MODEL), f32)
    norm_ab = gain(ks[1], (N_EVEN, D_MODEL))
    w_in_ab = nrm(ks[2], (N_EVEN, D_MODEL, 4 * D_A), D_MODEL ** -0.5)
    lru_conv_w = nrm(ks[3], (N_EVEN, A_CONV, D_A), A_CONV ** -0.5)
    lru_conv_b = nrm(ks[4], (N_EVEN, D_A), 0.02)
    lru_gate_r_w = nrm(ks[5], (N_EVEN, A_HEADS, A_HEAD_DIM, A_HEAD_DIM), A_HEAD_DIM ** -0.5)
    lru_gate_r_b = nrm(ks[6], (N_EVEN, D_A), 0.02)
    lru_gate_i_w = nrm(ks[7], (N_EVEN, A_HEADS, A_HEAD_DIM, A_HEAD_DIM), A_HEAD_DIM ** -0.5)
    lru_gate_i_b = nrm(ks[8], (N_EVEN, D_A), 0.02)
    a_pow = jax.random.uniform(ks[9], (N_EVEN, D_A), f32, minval=0.9, maxval=0.999)
    a_base = a_pow ** (1.0 / LRU_C)
    lru_lambda = jnp.log(a_base) - jnp.log1p(-a_base)
    sgu_ln_g = gain(ks[10], (N_EVEN, D_B))
    sgu_ln_b = nrm(ks[11], (N_EVEN, D_B), 0.02)
    sgu_w = nrm(ks[12], (N_EVEN, B_GROUPS, SGU_BLOCK, SGU_BLOCK), SGU_BLOCK ** -0.5)
    sgu_b = 1.0 + 0.02 * jax.random.normal(ks[13], (N_EVEN, B_GROUPS, SGU_BLOCK), f32)
    w_out_ab = nrm(ks[14], (N_EVEN, D_MIX, D_MODEL), D_MIX ** -0.5)
    norm_attn = gain(ks[15], (N_ODD, D_MODEL))
    w_qkv = nrm(ks[16], (N_ODD, D_MODEL, 3 * D_MODEL), D_MODEL ** -0.5)
    rel_bias = nrm(ks[17], (N_ODD, N_HEADS, N_REL), 0.1)
    w_o = nrm(ks[18], (N_ODD, D_MODEL, D_MODEL), D_MODEL ** -0.5)
    norm_ffn = gain(ks[19], (DEPTH, D_MODEL))
    ffn_w_up = nrm(ks[20], (DEPTH, D_MODEL, 2 * D_FF), D_MODEL ** -0.5)
    ffn_conv_w = nrm(ks[21], (DEPTH, FFN_CONV, 2 * D_FF), FFN_CONV ** -0.5)
    ffn_conv_b = nrm(ks[22], (DEPTH, 2 * D_FF), 0.02)
    ffn_w_down = nrm(ks[23], (DEPTH, D_FF, D_MODEL), D_FF ** -0.5)
    norm_final = gain(ks[24], (D_MODEL,))
    return {
        "x": x,
        "norm_ab": norm_ab, "w_in_ab": w_in_ab,
        "lru_conv_w": lru_conv_w, "lru_conv_b": lru_conv_b,
        "lru_gate_r_w": lru_gate_r_w, "lru_gate_r_b": lru_gate_r_b,
        "lru_gate_i_w": lru_gate_i_w, "lru_gate_i_b": lru_gate_i_b,
        "lru_lambda": lru_lambda,
        "sgu_ln_g": sgu_ln_g, "sgu_ln_b": sgu_ln_b, "sgu_w": sgu_w, "sgu_b": sgu_b,
        "w_out_ab": w_out_ab,
        "norm_attn": norm_attn, "w_qkv": w_qkv, "rel_bias": rel_bias, "w_o": w_o,
        "norm_ffn": norm_ffn, "ffn_w_up": ffn_w_up, "ffn_conv_w": ffn_conv_w,
        "ffn_conv_b": ffn_conv_b, "ffn_w_down": ffn_w_down,
        "norm_final": norm_final,
    }

def reference(x, norm_ab, w_in_ab, lru_conv_w, lru_conv_b, lru_gate_r_w, lru_gate_r_b,
              lru_gate_i_w, lru_gate_i_b, lru_lambda, sgu_ln_g, sgu_ln_b, sgu_w, sgu_b,
              w_out_ab, norm_attn, w_qkv, rel_bias, w_o, norm_ffn, ffn_w_up, ffn_conv_w,
              ffn_conv_b, ffn_w_down, norm_final):
    for layer in range(DEPTH):
        if layer % 2 == 0:
            e = layer // 2
            x = x + rglru_sgu_mixer(
                rms_norm(x, norm_ab[e]), w_in_ab[e], lru_conv_w[e], lru_conv_b[e],
                lru_gate_r_w[e], lru_gate_r_b[e], lru_gate_i_w[e], lru_gate_i_b[e],
                lru_lambda[e], sgu_ln_g[e], sgu_ln_b[e], sgu_w[e], sgu_b[e], w_out_ab[e])
        else:
            o = layer // 2
            x = x + chunk_band_attention(rms_norm(x, norm_attn[o]), w_qkv[o], rel_bias[o], w_o[o])
        x = x + conv_ffn(rms_norm(x, norm_ffn[layer]), ffn_w_up[layer], ffn_conv_w[layer],
                         ffn_conv_b[layer], ffn_w_down[layer])
    return rms_norm(x, norm_final)


_drawn_inputs = setup_inputs


def setup_inputs(seed=0):
    import zlib

    import numpy as np

    out = dict(_drawn_inputs(seed))
    spreads = {}
    factors = {'norm_ab': 3.057,
     'lru_gate_r_b': 8.0,
     'lru_gate_i_b': 8.0,
     'sgu_ln_g': 6.989,
     'sgu_ln_b': 6.815,
     'sgu_b': 6.027,
     'norm_attn': 8.0,
     'rel_bias': 6.536,
     'norm_ffn': 3.152,
     'ffn_conv_b': 3.122,
     'norm_final': 2.848}
    for name, (base, spread) in spreads.items():
        noise = np.random.default_rng([zlib.crc32(name.encode()), seed]).standard_normal(out[name].shape)
        drawn = base * np.exp(spread * noise) if base else spread * noise
        out[name] = __import__('jax').numpy.asarray(drawn.astype(out[name].dtype))
    for name, factor in factors.items():
        out[name] = (out[name] * factor).astype(out[name].dtype)
    return out
```

```python
from contextlib import ExitStack

import numpy as np

import concourse.bass as bass
from concourse import mybir

F32 = mybir.dt.float32
F32R = mybir.dt.float32r
ACT = mybir.ActivationFunctionType
ALU = mybir.AluOpType

P = 128
D = 1024
T = 512
KT = D // P
CHUNK = 64
HEADS, HD = 16, 64
PAIRS = HEADS // 2
MAX_REL = 256
D_A = 512
MT_A = D_A // P
A_CONV = 4
GROUPS = 8
D_FF = 2752
FF_PAIRS = D_FF // P
FF_TAIL = D_FF - FF_PAIRS * P
FF_KT = FF_PAIRS + 1
EPS = 1e-6
MASKED = 1e30

RAW = 6
RING = 3
UNIT = KT * P

U_AX, U_BV, U_GATES, U_BU, U_AG0, U_SGU, U_AG1 = 0, 4, 8, 9, 13, 14, 15
U_OUT = 18
U_UP = [U_OUT + KT, 0]
U_DOWN = [U_UP[0] + 2 * FF_PAIRS + 1, 0]
U_QKV = U_DOWN[0] + 3 * KT
U_WO = U_QKV + 3 * PAIRS
U_UP[1] = U_WO + KT
U_DOWN[1] = U_UP[1] + 2 * FF_PAIRS + 1
UNITS = U_DOWN[1] + 3 * KT
DOWN_KT = [8, 8, FF_KT - 16]

N_NORMS = 5
C_GAIN = 0
C_FFN = C_GAIN + N_NORMS * KT
FFN_COLS = FF_KT * 8
C_LRU = C_FFN + 2 * FFN_COLS
N_PARAMS = C_LRU + MT_A * 8

EXT = T + P
EXT_CLIP = T - MAX_REL - 1

STAT_BANK = 7
MIX_BANKS = [0, 1, 2, 5]
SIDE_BANKS = [6, 7, 3, 4]
UP_BANKS = [0, 1, 2, 5, 6, 7]
ATT_PROJ_BANKS = [0, 1]
SCORE_BANKS = [2, 3, 4]
TR_BANKS = [7, 6]
AV_BANK = 5
RES_BANKS = [[3, 4], [3, 4], [0, 1], [3, 4]]

Y_ORDER = [0, 4, 5, 6, 7, 1, 2, 3]

SCORE_GROUPS = [[(3, 0)], [(2, 0), (0, 384)], [(1, 0)]]
P_OFF = [0, 128, 384, 768]
P_COLS = 1280
TR_GROUPS = [[(0, 0), (1, 0), (2, 0), (3, 0)], [(1, 1), (2, 1), (3, 1), (3, 3)], [(2, 2), (3, 2)]]
TR_OFF = [0, 512, 1024]
KEY_OFF = [0, 512, 1024, 896]


class Steps:

    def __init__(self, sem):
        self.sem, self.n, self.turn, self.per = sem, 0, None, 0

    def enter(self, turn, per):
        self.turn, self.per, self.at = turn, per, self.n

    def leave(self, turns):
        assert self.n - self.at == self.per, (self.n - self.at, self.per)
        self.n, self.turn = self.at + turns * self.per, None

    def value(self):
        return self.n if self.turn is None else self.turn * self.per + self.n


def trunk(nc, x_in, weights, params, rel_rev, ln_g, ln_b, sgu_b, out):
    ctx = ExitStack()
    with ctx:
        def persistent(name, shape, dt):
            return ctx.enter_context(nc.sbuf_tensor(name, shape, dt))

        def sem(name):
            return ctx.enter_context(nc.semaphore(name))

        x = persistent("x", [P, KT, T], F32)
        xh = persistent("xh", [P, KT, T], F32R)
        xl = persistent("xl", [P, KT, T], F32R)
        raw = persistent("raw", [P, RAW, UNIT], F32)
        wh = persistent("wh", [P, RING, KT, P], F32R)
        wl = persistent("wl", [P, RING, KT, P], F32R)
        par = persistent("par", [P, N_PARAMS], F32)
        ident = persistent("ident", [P, P], F32)
        mean_w = persistent("mean_w", [P, P], F32R)
        rstd = persistent("rstd", [P, T], F32)
        acc = persistent("acc", [P, T], F32)
        acch = persistent("acch", [P, T], F32R)
        accl = persistent("accl", [P, T], F32R)
        sq = persistent("sq", [P, 2, T], F32)
        small = persistent("small", [P, 49], F32)
        eps = small[:, 0:1]
        idle = small[:, 1:2]
        neg_min = small[:, 2:10]
        psums = small[:, 10:18]
        lru_rate = small[:, 18:22]
        ln_mv = small[:, 22:30].rearrange("p (n c) -> p n c", c=2)
        ln_var = small[:, 30:34]
        ln_rstd = small[:, 34:38]
        ln_tmp = small[:, 38:42]
        idle2 = small[:, 42:43]
        gate_word = small[:, 43:49]
        bn6 = persistent("bn6", [P, 4, 6], F32)

        root, newt = sq[:, 0], sq[:, 1]

        with ExitStack() as phase:
            def mixer(name, shape, dt):
                return phase.enter_context(nc.sbuf_tensor(name, shape, dt))

            base_y = nc.sbuf_base
            yh = mixer("yh", [P, KT, T], F32R)
            yl = mixer("yl", [P, KT, T], F32R)
            decay = nc.alloc_sbuf_tensor_at("decay", [P, MT_A, T], F32, offset=base_y)
            expm = nc.alloc_sbuf_tensor_at("expm", [P, MT_A, T], F32, offset=base_y + KT * T * 4)
            mxh = mixer("mxh", [P, MT_A, T], F32R)
            mxl = mixer("mxl", [P, MT_A, T], F32R)
            axc = mixer("axc", [P, MT_A, T], F32)
            rec = mixer("rec", [P, MT_A, T], F32)
            vg = mixer("vg", [P, MT_A, T], F32)
            gu = mixer("gu", [P, MT_A, T], F32)
            lng = mixer("lng", [P, D_A], F32)
            lnb = mixer("lnb", [P, D_A], F32)
            sgb = mixer("sgb", [P, GROUPS // 2, P], F32)
            axp = mixer("axp", [P, A_CONV - 1 + T], F32)
            maskt = mixer("maskt", [CHUNK, HEADS, CHUNK], F32)
            relt = mixer("relt", [HEADS, 2 * MAX_REL + 1], F32)
            ext = mixer("ext", [HEADS, EXT], F32)

        with ExitStack() as phase:
            def ffn_mem(name, shape, dt):
                return phase.enter_context(nc.sbuf_tensor(name, shape, dt))

            ah = ffn_mem("ah", [P, FF_KT, T], F32R)
            al = ffn_mem("al", [P, FF_KT, T], F32R)
            ub = [ffn_mem(f"ub{i}", [P, 2 + T], F32) for i in range(2)]
            cg = ffn_mem("cg", [P, T], F32)
            cu = ffn_mem("cu", [P, T], F32)

        with ExitStack() as phase:
            def att_mem(name, shape, dt):
                return phase.enter_context(nc.sbuf_tensor(name, shape, dt))

            oh = att_mem("oh", [P, PAIRS, T], F32R)
            ol = att_mem("ol", [P, PAIRS, T], F32R)
            qh = att_mem("qh", [P, 2, T], F32R)
            ql = att_mem("ql", [P, 2, T], F32R)
            kh = att_mem("kh", [P, 2, T], F32R)
            kl = att_mem("kl", [P, 2, T], F32R)
            vh = att_mem("vh", [P, T], F32R)
            vl = att_mem("vl", [P, T], F32R)
            pth = att_mem("pth", [P, 2, P_COLS], F32R)
            ptl = att_mem("ptl", [P, 2, P_COLS], F32R)
            p_sb = att_mem("p_sb", [P, 2, P_COLS], F32)
            q_sb = att_mem("q_sb", [P, T], F32)
            k_sb = att_mem("k_sb", [P, T], F32)
            v_sb = att_mem("v_sb", [P, T], F32)
            bias = att_mem("bias", [P, 2, 2, T], F32)

        bank = [ctx.enter_context(nc.psum_tensor(f"bank{i}", [P, T], F32)) for i in range(8)]

        ext_d = nc.dram_tensor("ext_scratch", (HEADS, EXT), F32).ap()
        bias_d = nc.dram_tensor("bias_scratch", (HEADS, P, T), F32).ap()

        raw_in = [sem(f"raw_in{i}") for i in range(RAW)]
        x_in_sem = [sem(f"x_in{i}") for i in range(4)]
        par_in, rel_in, ext_out, bias_out = sem("par_in"), sem("rel_in"), sem("ext_out"), sem("bias_out")
        mask_out, ln_in, out_done = sem("mask_out"), sem("ln_in"), sem("out_done")
        bias_in = [sem(f"bias_in{i}") for i in range(2)]
        w_hi, w_lo, w_used = sem("w_hi"), sem("w_lo"), sem("w_used")
        x_ready, x_hi, x_lo, x_sq, x_acc = (sem(n) for n in ("x_ready", "x_hi", "x_lo", "x_sq", "x_acc"))
        acc_hi, acc_lo, stat_mm, root_done, rstd_done = (
            sem(n) for n in ("acc_hi", "acc_lo", "stat_mm", "root_done", "rstd_done"))
        dve_step, pool_step = sem("dve_step"), sem("pool_step")
        const_done, ident_done, maskt_done, ext_done = (
            sem(n) for n in ("const_done", "ident_done", "maskt_done", "ext_done"))
        lam_abs, lam_exp, mix_free, ax_conv, ax_hi, ax_lo, gelu_v = (
            sem(n) for n in ("lam_abs", "lam_exp", "mix_free", "ax_conv", "ax_hi", "ax_lo", "gelu_v"))
        gates_mm, gate_sig, ix_done, tanh_done, expm_done, expm_root = (
            sem(n) for n in ("gates_mm", "gate_sig", "ix_done", "tanh_done", "expm_done", "expm_root"))
        tr_mm, ln_var_done, ln_root, ln_norm, ln_affine, v_hi, v_lo = (
            sem(n) for n in ("tr_mm", "ln_var_done", "ln_root", "ln_norm", "ln_affine", "v_hi", "v_lo"))
        sgu_masked, sgu_mm, sgu_free, gelu_u, gelu_g, y_prod, y_hi, y_lo = (
            sem(n) for n in ("sgu_masked", "sgu_mm", "sgu_free", "gelu_u", "gelu_g", "y_prod", "y_hi", "y_lo"))
        up_free, conv_done, silu_done, prod_done, act_hi, act_lo = (
            [sem(f"{n}{layer}") for layer in range(2)]
            for n in ("up_free", "conv_done", "silu_done", "prod_done", "act_hi", "act_lo"))
        qkv_out, qk_hi, qk_lo, score_mm, score_out, exp_done, p_norm = (
            sem(n) for n in ("qkv_out", "qk_hi", "qk_lo", "score_mm", "score_out", "exp_done", "p_norm"))
        ptr_mm, ptr_hi, ptr_lo, av_mm, o_hi, o_lo, rsum_inv = (
            sem(n) for n in ("ptr_mm", "ptr_hi", "ptr_lo", "av_mm", "o_hi", "o_lo", "rsum_inv"))
        out_dve, out_pool = sem("out_dve"), sem("out_pool")

        def gain(norm, m):
            return par[:, bass.ds(m + (C_GAIN + norm * KT), 1)] if not isinstance(m, int) \
                else par[:, C_GAIN + norm * KT + m:C_GAIN + norm * KT + m + 1]

        def lru_par(m, k):
            return par[:, C_LRU + 8 * m + k:C_LRU + 8 * m + k + 1]

        def tile_of(buf, m):
            return buf[:, m] if isinstance(m, int) else buf[:, bass.ds(m, 1), :]

        block = ctx.enter_context(nc.Block())

        @block.sync
        def _(sp):
            def load_unit(c, turn=0):
                n = c + RAW * turn
                if c >= RAW or not isinstance(turn, int):
                    sp.wait_ge(w_lo, n - (RAW - 1))
                at = weights[n] if isinstance(n, int) else weights[bass.ds(n, 1)].rearrange("u p c -> (u p) c")
                sp.dma_start(raw[:, c % RAW, :], at).then_inc(raw_in[c % RAW], 16)

            sp.dma_start(par[:], params).then_inc(par_in, 16)
            for i in range(4):
                if i < 2:
                    load_unit(i)
                sp.dma_start(x[:, 2 * i:2 * i + 2], x_in[:, 2 * i:2 * i + 2]).then_inc(x_in_sem[i], 16)
            for c in range(2, RAW):
                load_unit(c)
            sp.dma_start(relt[:], rel_rev).then_inc(rel_in, 16)
            sp.dma_start(lng[:], bass.AP(ln_g.tensor, 0, [[0, P], [1, D_A]])).then_inc(ln_in, 16)
            sp.dma_start(lnb[:], bass.AP(ln_b.tensor, 0, [[0, P], [1, D_A]])).then_inc(ln_in, 16)
            for half in range(2):
                sp.dma_start(sgb[half * 64:half * 64 + 64],
                             bass.AP(sgu_b.tensor, half * P, [[0, 64], [2 * P, GROUPS // 2], [1, P]])
                             ).then_inc(ln_in, 16)
            for c in range(RAW, 2 * RAW):
                load_unit(c)
            sp.wait_ge(ext_done, 1)
            sp.dma_start(ext_d, ext[:]).then_inc(ext_out, 16)
            load_unit(2 * RAW)
            load_unit(2 * RAW + 1)
            sp.wait_ge(ext_out, 16)
            sp.dma_start(bias_d, bass.AP(ext_d.tensor, P - 1, [[EXT, HEADS], [-1, P], [1, T]])).then_inc(bias_out, 16)
            for c in range(2 * RAW + 2, 3 * RAW):
                load_unit(c)
            sp.wait_ge(bias_out, 16)
            sp.wait_ge(maskt_done, 1)
            sp.dma_start(bias_d[:, 0:CHUNK, T - CHUNK:T].rearrange("h p c -> p h c"), maskt[:]).then_inc(mask_out, 16)
            with sp.Fori(0, UNITS // RAW - 3) as turn:
                for c in range(3 * RAW, 4 * RAW):
                    load_unit(c, turn)
            for m in range(KT):
                if m % 2 == 0:
                    sp.wait_ge(out_dve, m // 2 + 1)
                else:
                    sp.wait_ge(out_pool, m // 2 + 1)
                sp.dma_start(out[:, m], x[:, m]).then_inc(out_done, 16)
            sp.wait_ge(out_done, 16 * KT)

        @block.gpsimd
        def _(pool):
            steps = Steps(pool_step)

            def link(ins):
                ins.then_inc(pool_step, 1)
                steps.n += 1
                pool.wait_ge(pool_step, steps.value())

            def split_lo(c, turn=0):
                pool.wait_ge(w_hi, c + 1 + RAW * turn)
                nc.gpsimd.tensor_tensor(
                    wl[:, c % RING].rearrange("p k c -> p (k c)"), raw[:, c % RAW],
                    wh[:, c % RING].rearrange("p k c -> p (k c)"), ALU.subtract).then_inc(w_lo, 1)

            nc.gpsimd.memset(eps, EPS).then_inc(const_done, 1)
            nc.gpsimd.memset(idle, 0.0).then_inc(const_done, 1)
            nc.gpsimd.memset(mean_w[:].bitcast(F32), 1.0 / D).then_inc(const_done, 1)
            split_lo(0)
            split_lo(1)
            link(nc.gpsimd.memset(ident[:], 0.0))
            nc.gpsimd.affine_select(out=ident[:], in_=ident[:], compare_op=ALU.not_equal, fill=1.0, base=0,
                                    pattern=[[-1, P]], channel_multiplier=1).then_inc(ident_done, 1)
            split_lo(2)
            nc.gpsimd.memset(maskt[:], MASKED).then_inc(maskt_done, 1)
            for c in range(3, U_AG0):
                split_lo(c)
            pool.wait_ge(raw_in[U_SGU % RAW], 16 * (U_SGU // RAW + 1))
            pool.wait_ge(w_lo, U_AG0)
            nc.gpsimd.memset(raw[CHUNK:P, U_SGU % RAW].rearrange("p (g i) -> p g i", g=GROUPS)[:, :, 0:CHUNK],
                             0.0).then_inc(sgu_masked, 1)
            pool.wait_ge(sgu_masked, 1)
            split_lo(U_AG0)
            pool.wait_ge(ln_in, 16 * 4)
            for n in range(4):
                pool.wait_ge(ln_norm, n + 1)
                link(nc.gpsimd.tensor_tensor(vg[:, n], vg[:, n], lng[:], ALU.mult))
                nc.gpsimd.tensor_tensor(vg[:, n], vg[:, n], lnb[:], ALU.add).then_inc(ln_affine, 1)
            for c in range(U_SGU, 3 * RAW):
                split_lo(c)
            with pool.Fori(0, UNITS // RAW - 3) as turn:
                for c in range(3 * RAW, 4 * RAW):
                    split_lo(c, turn)
            pool.wait_ge(rstd_done, 5)
            pool.wait_ge(x_hi, 5 * KT)
            for m in range(1, KT, 2):
                nc.gpsimd.tensor_tensor(x[:, m], x[:, m], rstd[:], ALU.mult).then_inc(out_pool, 1)

        @block.scalar
        def _(act):
            def split_hi(c, turn=0):
                if c >= UNITS:
                    return
                act.wait_ge(raw_in[c % RAW], 16 * (c // RAW + 1) + 16 * turn)
                if c == U_SGU:
                    act.wait_ge(sgu_masked, 1)
                if c >= RING:
                    act.wait_ge(w_used, c - (RING - 1) + RAW * turn)
                nc.scalar.activation(wh[:, c % RING].rearrange("p k c -> p (k c)"), raw[:, c % RAW],
                                     ACT.Copy).then_inc(w_hi, 1)

            def norm_tile(norm, m, even):
                xm = tile_of(x, m)
                if norm or m >= 2:
                    act.wait_ge(x_acc, norm * KT + m - 1)
                if norm < 4:
                    nc.scalar.activation(tile_of(xh, m), xm, ACT.Copy, scale=gain(norm, m)).then_inc(x_hi, 1)
                nc.scalar.activation(tile_of(sq, even) if isinstance(m, int) else sq[:, even:even + 1, :],
                                     xm, ACT.Square).then_inc(x_sq, 1)
                if norm == 4:
                    nc.scalar.activation(xm, xm, ACT.Copy, scale=gain(norm, m)).then_inc(x_hi, 1)

            def statistics(norm):
                act.wait_ge(x_acc, (norm + 1) * KT)
                nc.scalar.activation(acch[:], acc[:], ACT.Copy).then_inc(acc_hi, 1)
                act.wait_ge(stat_mm, norm + 1)
                nc.scalar.activation(root, bank[STAT_BANK][:], ACT.Sqrt, bias=eps).then_inc(root_done, 1)

            def preload(func):
                nc.scalar.activation(idle2, idle, func)

            act.wait_ge(par_in, 16)
            act.wait_ge(const_done, 3)
            act.wait_ge(lam_abs, 1)
            nc.scalar.activation(ln_tmp, ln_var, ACT.Exp, scale=-1.0).then_inc(lam_exp, 1)
            for m in range(KT):
                if m % 2 == 0:
                    act.wait_ge(x_in_sem[m // 2], 16)
                norm_tile(0, m, m % 2)
                if m in (0, 2, 4):
                    split_hi(m // 2)
            statistics(0)
            for m in range(MT_A):
                split_hi(U_AX + m + 3)
                act.wait_ge(ax_conv, m + 1)
                nc.scalar.activation(mxh[:, m], axc[:, m], ACT.Copy).then_inc(ax_hi, 1)
            for m in range(MT_A):
                split_hi(U_BV + m + 3)
                act.wait_ge(mix_free, MT_A + m + 1)
                nc.scalar.activation(vg[:, m], vg[:, m], ACT.Gelu_apprx_tanh).then_inc(gelu_v, 1)
            for item in range(2 * MT_A):
                m = item // 2
                if item < 2 * MT_A - 1:
                    act.wait_ge(gates_mm, item + 1)
                else:
                    act.wait_ge(w_used, U_GATES + 1)
                nc.scalar.activation((expm if item % 2 else rec)[:, m], bank[SIDE_BANKS[item % 4]][:],
                                     ACT.Sigmoid, bias=lru_par(m, 5 + item % 2)).then_inc(gate_sig, 1)
            split_hi(U_GATES + 3)
            act.wait_ge(gate_sig, 2 * MT_A)
            act.wait_ge(dve_step, LRU_STEPS)
            for m in range(MT_A):
                nc.scalar.activation(decay[:, m], rec[:, m], ACT.Exp, scale=lru_rate[:, m:m + 1])
                act.wait_ge(ix_done, m + 1)
                nc.scalar.activation(expm[:, m], rec[:, m], ACT.Tanh, scale=lru_rate[:, m:m + 1]).then_inc(tanh_done, 1)
            split_hi(U_BU + 3)
            for m in range(MT_A):
                act.wait_ge(expm_done, m + 1)
                nc.scalar.activation(expm[:, m], expm[:, m], ACT.Sqrt, scale=-1.0).then_inc(expm_root, 1)
            act.wait_ge(ln_var_done, 1)
            nc.scalar.activation(ln_rstd, ln_var, ACT.Sqrt).then_inc(ln_root, 1)
            split_hi(U_BU + 4)
            for n in range(4):
                act.wait_ge(ln_affine, n + 1)
                nc.scalar.activation(mxh[:, n], vg[:, n], ACT.Copy).then_inc(v_hi, 1)
            split_hi(U_BU + 5)
            for m in range(MT_A):
                act.wait_ge(mix_free, 2 * MT_A + m + 1)
                nc.scalar.activation(gu[:, m], gu[:, m], ACT.Gelu_apprx_tanh).then_inc(gelu_u, 1)
                if m == 2:
                    split_hi(U_BU + 6)

            def gelu_gate(m):
                act.wait_ge(mix_free, 3 * MT_A + m + 1)
                nc.scalar.activation(axp[:, 0:T], axp[:, 0:T], ACT.Gelu_apprx_tanh).then_inc(gelu_g, 1)

            def split_y(s):
                act.wait_ge(y_prod, s + 1)
                src = rec if Y_ORDER[s] < MT_A else vg
                nc.scalar.activation(yh[:, Y_ORDER[s]], src[:, Y_ORDER[s] % MT_A], ACT.Copy).then_inc(y_hi, 1)

            gelu_gate(0)
            split_y(0)
            split_hi(U_AG0 + 3)
            for s in range(1, 5):
                split_y(s)
            split_hi(U_SGU + 3)
            for m in range(1, MT_A):
                split_hi(U_AG1 + m - 1 + 3)
                gelu_gate(m)
                split_y(4 + m)

            def residual_tiles(first_unit, stage):
                for m in range(KT):
                    split_hi(first_unit + m + 3)
                    act.wait_ge(x_ready, stage * KT + m + 1)
                    norm_tile(stage + 1, m, m % 2)
                statistics(stage + 1)

            def ffn(layer):
                preload(ACT.Silu)
                base = U_UP[layer]

                def gate_up(j, turn):
                    split_hi(base + 2 * j + 3, turn)
                    act.wait_ge(conv_done[layer], 2 * j + 1 + RAW * turn)
                    nc.scalar.activation(cg[:], cg[:], ACT.Silu).then_inc(silu_done[layer], 1)
                    split_hi(base + 2 * j + 4, turn)
                    act.wait_ge(prod_done[layer], j + 1 + 3 * turn)
                    nc.scalar.activation(tile_of(ah, j + 3 * turn), cu[:] if isinstance(turn, int) else
                                         cu[:].rearrange("p (a t) -> p a t", a=1), ACT.Copy).then_inc(act_hi[layer], 1)

                with act.Fori(0, FF_PAIRS // 3) as turn:
                    for j in range(3):
                        gate_up(j, turn)
                split_hi(base + 2 * FF_PAIRS + 3)
                act.wait_ge(conv_done[layer], 2 * FF_PAIRS + 1)
                nc.scalar.activation(cg[0:FF_TAIL], cg[0:FF_TAIL], ACT.Silu).then_inc(silu_done[layer], 1)
                act.wait_ge(prod_done[layer], FF_KT)
                nc.scalar.activation(ah[0:FF_TAIL, FF_PAIRS], cu[0:FF_TAIL], ACT.Copy).then_inc(act_hi[layer], 1)

                base = U_DOWN[layer]
                stage = 1 + 2 * layer

                def down(mm, turn):
                    for u in range(3):
                        split_hi(base + 3 * mm + u + 3, turn)
                    act.wait_ge(x_ready, stage * KT + mm + 1 + 2 * turn)
                    norm_tile(stage + 1, mm + 2 * turn, mm)

                with act.Fori(0, KT // 2 - 1) as turn:
                    for mm in range(2):
                        down(mm, turn)
                for mm in range(2):
                    down_last = KT - 2 + mm
                    for u in range(3):
                        split_hi(base + 3 * down_last + u + 3)
                    act.wait_ge(x_ready, stage * KT + down_last + 1)
                    norm_tile(stage + 1, down_last, mm)
                statistics(stage + 1)

            residual_tiles(U_OUT, 0)
            ffn(0)

            preload(ACT.Exp)
            act.wait_ge(mask_out, 16)

            def load_bias(c, turn=0):
                pair2 = 2 * c + 4 * turn
                if c >= 2:
                    act.wait_ge(score_out, 8 * (c - 1) + 16 * turn)
                src = bias_d[pair2:pair2 + 2] if isinstance(turn, int) else bias_d[bass.ds(pair2, 2)]
                act.dma_start(bias[:, c % 2], src.rearrange("h p t -> p h t")).then_inc(bias_in[c % 2], 16)

            def split_qk(c, turn, which):
                act.wait_ge(qkv_out, 3 * c + which + 1 + 6 * turn)
                nc.scalar.activation((kh if which else qh)[:, c % 2], (k_sb if which else q_sb)[:],
                                     ACT.Copy).then_inc(qk_hi, 1)

            def exponentials(c, turn, hh):
                head = 2 * c + hh
                for s, i in enumerate((3, 2, 0, 1)):
                    act.wait_ge(score_out, 4 * head + s + 1 + 16 * turn)
                    blk = p_sb[:, hh, P_OFF[i]:P_OFF[i] + P * (i + 1)]
                    nc.scalar.activation(blk, blk, ACT.Exp, scale=-1.0, bias=neg_min[:, 4 * hh + i:4 * hh + i + 1],
                                         accum_out=psums[:, 4 * hh + i:4 * hh + i + 1]).then_inc(exp_done, 1)

            def split_transposed(c, turn, t):
                act.wait_ge(ptr_mm, 7 * c + t + 1 + 14 * turn)
                src = bank[TR_BANKS[(c + t) % 2]]
                if t == 0:
                    nc.scalar.activation(vh[:], src[:], ACT.Copy).then_inc(ptr_hi, 1)
                    return
                hh, g = (t - 1) // 3, (t - 1) % 3
                if g == 0 and (c >= 1 or not isinstance(turn, int)):
                    act.wait_ge(av_mm, 2 * c + hh - 1 + 4 * turn)
                n = P * len(TR_GROUPS[g])
                nc.scalar.activation(pth[:, hh, TR_OFF[g]:TR_OFF[g] + n], src[:, 0:n], ACT.Copy).then_inc(ptr_hi, 1)

            def split_o(c, turn, hh):
                act.wait_ge(av_mm, 2 * c + hh + 1 + 4 * turn)
                half = slice(HD * hh, HD * hh + HD)
                pair = c + 2 * turn
                dst = oh[half, pair] if isinstance(turn, int) else oh[half, bass.ds(pair, 1), :]
                src = bank[AV_BANK][half, :]
                nc.scalar.activation(dst, src if isinstance(turn, int) else src.rearrange("p (a t) -> p a t", a=1),
                                     ACT.Copy).then_inc(o_hi, 1)

            def attend(c, turn, following):
                unit = U_QKV + 3 * (c + 1)
                if following:
                    load_bias(c + 1, turn)
                split_transposed(c, turn, 0)
                exponentials(c, turn, 0)
                if following:
                    split_hi(unit + 3, turn)
                    split_qk(c + 1, turn, 0)
                exponentials(c, turn, 1)
                split_transposed(c, turn, 1)
                split_transposed(c, turn, 2)
                split_transposed(c, turn, 3)
                if following:
                    split_hi(unit + 4, turn)
                    split_qk(c + 1, turn, 1)
                split_o(c, turn, 0)
                for t in (4, 5, 6):
                    split_transposed(c, turn, t)
                if following:
                    split_hi(unit + 5, turn)
                split_o(c, turn, 1)

            load_bias(0)
            split_hi(U_QKV + 3)
            split_qk(0, 0, 0)
            split_hi(U_QKV + 4)
            split_qk(0, 0, 1)
            split_hi(U_QKV + 5)
            attend(0, 0, True)
            attend(1, 0, True)
            with act.Fori(0, PAIRS // 2 - 2) as turn:
                attend(2, turn, True)
                attend(3, turn, True)
            attend(PAIRS - 2, 0, True)
            attend(PAIRS - 1, 0, False)
            residual_tiles(U_WO, 2)
            ffn(1)

        @block.vector
        def _(dve):
            steps = Steps(dve_step)

            def link(ins):
                ins.then_inc(dve_step, 1)
                steps.n += 1
                dve.wait_ge(dve_step, steps.value())

            stt = nc.vector.scalar_tensor_tensor
            tt = nc.vector.tensor_tensor
            ts = nc.vector.tensor_scalar

            def norm_tile(norm, m, even):
                if norm < 4:
                    dve.wait_ge(x_hi, norm * KT + m + 1)
                    stt(tile_of(xl, m), tile_of(x, m), gain(norm, m), tile_of(xh, m),
                        ALU.mult, ALU.subtract).then_inc(x_lo, 1)
                dve.wait_ge(x_sq, norm * KT + m + 1)
                if norm or m:
                    dve.wait_ge(x_acc, norm * KT + m)
                tt(acc[:], acc[:], sq[:, even], ALU.add).then_inc(x_acc, 1)

            def statistics(norm):
                dve.wait_ge(acc_hi, norm + 1)
                tt(accl[:], acc[:], acch[:], ALU.subtract).then_inc(acc_lo, 1)
                dve.wait_ge(root_done, norm + 1)
                link(nc.vector.reciprocal(rstd[:], root))
                link(tt(newt, rstd[:], rstd[:], ALU.mult))
                link(stt(newt, bank[STAT_BANK][:], EPS, newt, ALU.add, ALU.mult))
                link(ts(newt, newt, -0.5, 1.5, ALU.mult, ALU.add))
                tt(rstd[:], rstd[:], newt, ALU.mult).then_inc(rstd_done, 1)
                dve.wait_ge(rstd_done, norm + 1)
                if norm < 4:
                    link(nc.vector.memset(acc[:], 0.0))

            lam = par[:, C_LRU:C_LRU + 8 * MT_A].rearrange("p (m k) -> p m k", k=8)[:, :, 7]
            dve.wait_ge(par_in, 16)
            link(ts(ln_rstd, lam, -1.0, None, ALU.mult))
            tt(ln_var, lam, ln_rstd, ALU.max).then_inc(lam_abs, 1)
            dve.wait_ge(lam_exp, 1)
            link(ts(ln_var, ln_tmp, 2.0, None, ALU.add))
            link(nc.vector.reciprocal(ln_var, ln_var))
            link(tt(ln_tmp, ln_tmp, ln_var, ALU.mult))
            link(tt(ln_var, ln_tmp, ln_tmp, ALU.mult))
            link(ts(lru_rate, ln_var, 1.0 / 17, None, ALU.mult))
            for k in range(15, 2, -2):
                link(stt(lru_rate, lru_rate, 1.0 / k, ln_var, ALU.add, ALU.mult))
            link(stt(lru_rate, lru_rate, 1.0, ln_tmp, ALU.add, ALU.mult))
            link(ts(ln_rstd, ln_rstd, 0.0, None, ALU.max))
            link(stt(lru_rate, lru_rate, 2.0, ln_rstd, ALU.mult, ALU.add))
            link(ts(lru_rate, lru_rate, -8.0, None, ALU.mult))
            assert steps.n == LRU_STEPS, steps.n
            link(nc.vector.memset(acc[:], 0.0))
            link(nc.vector.memset(axp[:, 0:A_CONV - 1], 0.0))

            for m in range(KT):
                norm_tile(0, m, m % 2)
            dve.wait_ge(rel_in, 16)
            link(ts(ext[:, 0:EXT_CLIP], relt[:, 0:1].to_broadcast([HEADS, EXT_CLIP]), -1.0, None, ALU.mult))
            ts(ext[:, EXT_CLIP:EXT], relt[:, 0:EXT - EXT_CLIP], -1.0, None, ALU.mult).then_inc(ext_done, 1)
            statistics(0)

            def scaled_out(unit, dst):
                index = unit if unit < U_GATES else unit - 1 if unit <= U_AG0 else unit - 2
                dve.wait_ge(w_used, unit + 1)
                tt(dst, bank[MIX_BANKS[index % 4]][:], rstd[:], ALU.mult).then_inc(mix_free, 1)
                dve.wait_ge(mix_free, index + 1)

            def conv_lo(m):
                dve.wait_ge(ax_hi, m + 1)
                tt(mxl[:, m], axc[:, m], mxh[:, m], ALU.subtract).then_inc(ax_lo, 1)

            for m in range(MT_A):
                if m:
                    dve.wait_ge(ax_conv, m)
                scaled_out(U_AX + m, axp[:, A_CONV - 1:])
                link(ts(axc[:, m], axp[:, 3:3 + T], lru_par(m, 3), lru_par(m, 4), ALU.mult, ALU.add))
                link(stt(axc[:, m], axp[:, 2:2 + T], lru_par(m, 2), axc[:, m], ALU.mult, ALU.add))
                link(stt(axc[:, m], axp[:, 1:1 + T], lru_par(m, 1), axc[:, m], ALU.mult, ALU.add))
                stt(axc[:, m], axp[:, 0:T], lru_par(m, 0), axc[:, m], ALU.mult, ALU.add).then_inc(ax_conv, 1)
                if m:
                    conv_lo(m - 1)
            conv_lo(MT_A - 1)
            for m in range(MT_A):
                scaled_out(U_BV + m, vg[:, m])
            for m in range(MT_A):
                dve.wait_ge(gate_sig, 2 * m + 2)
                tt(axc[:, m], axc[:, m], expm[:, m], ALU.mult).then_inc(ix_done, 1)
            for m in range(MT_A):
                dve.wait_ge(tanh_done, m + 1)
                link(tt(rec[:, m], decay[:, m], decay[:, m], ALU.mult))
                stt(expm[:, m], rec[:, m], 1.0, expm[:, m], ALU.add, ALU.mult).then_inc(expm_done, 1)
            for n in range(4):
                dve.wait_ge(tr_mm, n + 1)
                link(nc.vector.bn_stats(bn6[:, n], bank[SIDE_BANKS[n]][:]))
                link(nc.vector.bn_aggr(ln_mv[:, n], bn6[:, n]))
            ts(ln_var, ln_mv[:, :, 1], EPS, None, ALU.add).then_inc(ln_var_done, 1)
            dve.wait_ge(ln_root, 1)
            link(nc.vector.reciprocal(ln_rstd, ln_rstd))
            link(tt(ln_tmp, ln_rstd, ln_rstd, ALU.mult))
            link(tt(ln_tmp, ln_tmp, ln_var, ALU.mult))
            link(ts(ln_tmp, ln_tmp, -0.5, 1.5, ALU.mult, ALU.add))
            link(tt(ln_rstd, ln_rstd, ln_tmp, ALU.mult))
            for n in range(4):
                ts(vg[:, n], bank[SIDE_BANKS[n]][:], ln_mv[:, n, 0:1], ln_rstd[:, n:n + 1],
                   ALU.subtract, ALU.mult).then_inc(ln_norm, 1)

            def recurrence(m):
                dve.wait_ge(expm_root, m + 1)
                link(tt(expm[:, m], expm[:, m], axc[:, m], ALU.mult))
                link(nc.vector.tensor_tensor_scan(rec[:, m], decay[:, m], expm[:, m], 0.0, ALU.mult, ALU.add))

            def v_split_lo(n):
                dve.wait_ge(v_hi, n + 1)
                tt(mxl[:, n], vg[:, n], mxh[:, n], ALU.subtract).then_inc(v_lo, 1)

            scaled_out(U_BU, gu[:, 0])
            recurrence(0)
            v_split_lo(0)
            v_split_lo(1)
            recurrence(1)
            v_split_lo(2)
            v_split_lo(3)
            scaled_out(U_BU + 1, gu[:, 1])
            scaled_out(U_BU + 2, gu[:, 2])
            recurrence(2)
            scaled_out(U_BU + 3, gu[:, 3])
            recurrence(3)

            def gated(m):
                scaled_out(U_AG0 if m == 0 else U_AG1 + m - 1, axp[:, 0:T])
                dve.wait_ge(gelu_g, m + 1)
                tt(rec[:, m], rec[:, m], axp[:, 0:T], ALU.mult).then_inc(y_prod, 1)

            def y_split_lo(s):
                src = rec if Y_ORDER[s] < MT_A else vg
                dve.wait_ge(y_hi, s + 1)
                tt(yl[:, Y_ORDER[s]], src[:, Y_ORDER[s] % MT_A], yh[:, Y_ORDER[s]], ALU.subtract).then_inc(y_lo, 1)

            gated(0)
            y_split_lo(0)
            for gp in range(GROUPS // 2):
                for half in range(2):
                    item = 2 * gp + half
                    if item < GROUPS - 1:
                        dve.wait_ge(sgu_mm, item + 1)
                    else:
                        dve.wait_ge(w_used, U_SGU + 1)
                    ps = bank[SIDE_BANKS[item % 4]][:].rearrange("p (n g i) -> p n g i", n=2, g=2)
                    for g in range(2):
                        rows = slice(64 * g, 64 * g + 64)
                        ins = tt(vg[rows, gp, half * 256:half * 256 + 256].rearrange("p (n i) -> p n i", n=2),
                                 ps[rows, :, g, :], sgb[rows, gp:gp + 1, :].to_broadcast([64, 2, P]), ALU.add)
                        if g:
                            ins.then_inc(sgu_free, 1)
                        else:
                            link(ins)
                dve.wait_ge(sgu_free, 2 * gp + 2)
                dve.wait_ge(gelu_u, gp + 1)
                tt(vg[:, gp], vg[:, gp], gu[:, gp], ALU.mult).then_inc(y_prod, 1)
                if gp:
                    y_split_lo(gp)
            y_split_lo(4)
            for m in range(1, MT_A):
                gated(m)
                y_split_lo(4 + m)

            def residual_tiles(first_unit, stage):
                for m in range(KT):
                    dve.wait_ge(w_used, first_unit + m + 1)
                    tt(x[:, m], x[:, m], bank[RES_BANKS[stage][m % 2]][:], ALU.add).then_inc(x_ready, 1)
                    norm_tile(stage + 1, m, m % 2)
                statistics(stage + 1)

            def ffn(layer):
                base = U_UP[layer]
                for b in ub:
                    link(nc.vector.memset(b[:, 0:2], 0.0))

                def conv(t, turn, u, c, at):
                    dve.wait_ge(w_used, base + t + 1 + RAW * turn)
                    tt(u[:, 2:], bank[UP_BANKS[t % 6]][:], rstd[:], ALU.mult).then_inc(up_free[layer], 1)
                    dve.wait_ge(up_free[layer], t + 1 + RAW * turn)
                    tap = [par[:, bass.ds(at + k, 1)] if not isinstance(at, int) else par[:, at + k:at + k + 1]
                           for k in range(4)]
                    link(ts(c[:], u[:, 2:2 + T], tap[2], tap[3], ALU.mult, ALU.add))
                    link(stt(c[:], u[:, 1:1 + T], tap[1], c[:], ALU.mult, ALU.add))
                    stt(c[:], u[:, 0:T], tap[0], c[:], ALU.mult, ALU.add).then_inc(conv_done[layer], 1)

                cols = C_FFN + layer * FFN_COLS
                with dve.Fori(0, FF_PAIRS // 3) as turn:
                    steps.enter(turn, 12)
                    for j in range(3):
                        conv(2 * j, turn, ub[0], cg, cols + 8 * j + 24 * turn)
                        conv(2 * j + 1, turn, ub[1], cu, cols + 8 * j + 4 + 24 * turn)
                        dve.wait_ge(silu_done[layer], j + 1 + 3 * turn)
                        dve.wait_ge(conv_done[layer], 2 * j + 2 + 6 * turn)
                        tt(cu[:], cg[:], cu[:], ALU.mult).then_inc(prod_done[layer], 1)
                        dve.wait_ge(act_hi[layer], j + 1 + 3 * turn)
                        pair = j + 3 * turn
                        tt(al[:, bass.ds(pair, 1), :], cu[:].rearrange("p (a t) -> p a t", a=1),
                           ah[:, bass.ds(pair, 1), :], ALU.subtract).then_inc(act_lo[layer], 1)
                        dve.wait_ge(act_lo[layer], pair + 1)
                    steps.leave(FF_PAIRS // 3)
                conv(2 * FF_PAIRS, 0, ub[0], cg, cols + 8 * FF_PAIRS)
                dve.wait_ge(conv_done[layer], 2 * FF_PAIRS + 1)
                link(nc.vector.tensor_copy(cu[0:FF_TAIL], cg[FF_TAIL:P]))
                dve.wait_ge(silu_done[layer], FF_KT)
                tt(cu[0:FF_TAIL], cg[0:FF_TAIL], cu[0:FF_TAIL], ALU.mult).then_inc(prod_done[layer], 1)
                dve.wait_ge(act_hi[layer], FF_KT)
                tt(al[0:FF_TAIL, FF_PAIRS], cu[0:FF_TAIL], ah[0:FF_TAIL, FF_PAIRS],
                   ALU.subtract).then_inc(act_lo[layer], 1)

                stage = 1 + 2 * layer
                base_d = U_DOWN[layer]
                with dve.Fori(0, KT // 2) as turn:
                    for mm in range(2):
                        dve.wait_ge(w_used, base_d + 3 * mm + 3 + RAW * turn)
                        xm = x[:, bass.ds(mm + 2 * turn, 1), :]
                        tt(xm, xm, bank[RES_BANKS[stage][mm]][:].rearrange("p (a t) -> p a t", a=1),
                           ALU.add).then_inc(x_ready, 1)
                        norm_tile(stage + 1, mm + 2 * turn, mm)
                statistics(stage + 1)

            residual_tiles(U_OUT, 0)
            ffn(0)

            def qkv_evacuate(c, turn, which):
                dve.wait_ge(w_used, U_QKV + 3 * c + which + 1 + RAW * turn)
                ps = bank[ATT_PROJ_BANKS[(c + which) % 2]]
                if which == 0:
                    stt(q_sb[:], ps[:], -(HD ** -0.5), rstd[:], ALU.mult, ALU.mult).then_inc(qkv_out, 1)
                else:
                    tt((k_sb, v_sb)[which - 1][:], ps[:], rstd[:], ALU.mult).then_inc(qkv_out, 1)

            def qk_split_lo(c, turn, which):
                dve.wait_ge(qk_hi, 2 * c + which + 1 + 4 * turn)
                hi, lo, src = (kh, kl, k_sb) if which else (qh, ql, q_sb)
                tt(lo[:, c % 2], src[:], hi[:, c % 2], ALU.subtract).then_inc(qk_lo, 1)

            def scores(c, turn, hh):
                head = 2 * c + hh
                s = 0
                if hh == 0:
                    dve.wait_ge(bias_in[c % 2], 16 * (c // 2 + 1) + 16 * turn)
                if c >= 1 or not isinstance(turn, int):
                    dve.wait_ge(ptr_mm, 7 * (c - 1) + 3 * hh + 4 + 14 * turn)
                for g, group in enumerate(SCORE_GROUPS):
                    dve.wait_ge(score_mm, 3 * head + g + 1 + 12 * turn)
                    nc.vector.memset(gate_word[:, 3 * hh + g:3 * hh + g + 1], 0.0)
                    for i, col in group:
                        n = P * (i + 1)
                        nc.vector.tensor_tensor_reduce(
                            out=p_sb[:, hh, P_OFF[i]:P_OFF[i] + n],
                            in0=bank[SCORE_BANKS[g]][:, col:col + n], in1=bias[:, c % 2, hh, T - n:T],
                            scale=1.0, scalar=3.0e38, op0=ALU.add, op1=ALU.min,
                            accum_out=neg_min[:, 4 * hh + i:4 * hh + i + 1]).then_inc(score_out, 1)
                        s += 1

            def normalise(c, turn, hh):
                head = 2 * c + hh
                for s, i in enumerate((3, 2, 0, 1)):
                    dve.wait_ge(exp_done, 4 * head + s + 1 + 16 * turn)
                    r = psums[:, 4 * hh + i:4 * hh + i + 1]
                    nc.vector.reciprocal(r, r).then_inc(rsum_inv, 1)
                    dve.wait_ge(rsum_inv, 4 * head + s + 1 + 16 * turn)
                    blk = p_sb[:, hh, P_OFF[i]:P_OFF[i] + P * (i + 1)]
                    ts(blk, blk, r, None, ALU.mult).then_inc(p_norm, 1)

            def transposed_split_lo(c, turn, t):
                dve.wait_ge(ptr_hi, 7 * c + t + 1 + 14 * turn)
                src = bank[TR_BANKS[(c + t) % 2]]
                if t == 0:
                    tt(vl[:], src[:], vh[:], ALU.subtract).then_inc(ptr_lo, 1)
                    return
                hh, g = (t - 1) // 3, (t - 1) % 3
                n = P * len(TR_GROUPS[g])
                tt(ptl[:, hh, TR_OFF[g]:TR_OFF[g] + n], src[:, 0:n], pth[:, hh, TR_OFF[g]:TR_OFF[g] + n],
                   ALU.subtract).then_inc(ptr_lo, 1)

            def o_split_lo(c, turn, hh):
                dve.wait_ge(o_hi, 2 * c + hh + 1 + 4 * turn)
                half = slice(HD * hh, HD * hh + HD)
                pair = c + 2 * turn
                src = bank[AV_BANK][half, :]
                if isinstance(turn, int):
                    tt(ol[half, pair], src, oh[half, pair], ALU.subtract).then_inc(o_lo, 1)
                else:
                    tt(ol[half, bass.ds(pair, 1), :], src.rearrange("p (a t) -> p a t", a=1),
                       oh[half, bass.ds(pair, 1), :], ALU.subtract).then_inc(o_lo, 1)

            def attend(c, turn, following):
                transposed_split_lo(c, turn, 0)
                scores(c, turn, 0)
                normalise(c, turn, 0)
                if following:
                    qkv_evacuate(c + 1, turn, 0)
                scores(c, turn, 1)
                if following:
                    qk_split_lo(c + 1, turn, 0)
                normalise(c, turn, 1)
                transposed_split_lo(c, turn, 1)
                transposed_split_lo(c, turn, 2)
                transposed_split_lo(c, turn, 3)
                if following:
                    qkv_evacuate(c + 1, turn, 1)
                    qk_split_lo(c + 1, turn, 1)
                o_split_lo(c, turn, 0)
                for t in (4, 5, 6):
                    transposed_split_lo(c, turn, t)
                if following:
                    qkv_evacuate(c + 1, turn, 2)
                o_split_lo(c, turn, 1)

            for which in range(3):
                qkv_evacuate(0, 0, which)
                if which < 2:
                    qk_split_lo(0, 0, which)
            attend(0, 0, True)
            attend(1, 0, True)
            with dve.Fori(0, PAIRS // 2 - 2) as turn:
                attend(2, turn, True)
                attend(3, turn, True)
            attend(PAIRS - 2, 0, True)
            attend(PAIRS - 1, 0, False)
            residual_tiles(U_WO, 2)
            ffn(1)

            dve.wait_ge(x_hi, 5 * KT)
            for m in range(0, KT, 2):
                tt(x[:, m], x[:, m], rstd[:], ALU.mult).then_inc(out_dve, 1)

        @block.tensor
        def _(pe):
            def product(dst, w_hi_part, w_lo_part, m_hi, m_lo, first, last):
                nc.tensor.matmul(dst, w_hi_part, m_hi, start=first, stop=False)
                nc.tensor.matmul(dst, w_hi_part, m_lo, start=False, stop=False)
                return nc.tensor.matmul(dst, w_lo_part, m_hi, start=False, stop=last)

            def tiles(dst, unit, ks, first, last, src=(None, None)):
                mh, ml = src
                slot = unit % RING
                for n, k in enumerate(ks):
                    ins = product(dst, wh[:, slot, k], wl[:, slot, k], mh[:, k], ml[:, k],
                                  first and n == 0, last and n == len(ks) - 1)
                return ins

            def whole(unit, b, turn=0, src=None):
                pe.wait_ge(w_lo, unit + 1 + RAW * turn)
                tiles(bank[b][:], unit, range(KT), True, True, src or (xh, xl)).then_inc(w_used, 1)

            def first_units(unit, banks, norm):
                a, b = bank[banks[0]][:], bank[banks[1]][:]
                src = (xh, xl)
                pe.wait_ge(w_lo, unit + 1)
                for k in range(KT - 1):
                    pe.wait_ge(x_lo, norm * KT + k + 1)
                    tiles(a, unit, [k], k == 0, False, src)
                pe.wait_ge(w_lo, unit + 2)
                tiles(b, unit + 1, range(4), True, False, src)
                statistics(norm)
                tiles(b, unit + 1, range(4, KT - 1), False, False, src)
                pe.wait_ge(x_lo, (norm + 1) * KT)
                tiles(a, unit, [KT - 1], False, True, src).then_inc(w_used, 1)
                tiles(b, unit + 1, [KT - 1], False, True, src).then_inc(w_used, 1)

            def statistics(norm):
                pe.wait_ge(acc_lo, norm + 1)
                nc.tensor.matmul(bank[STAT_BANK][:], mean_w[:], acch[:], start=True, stop=False)
                nc.tensor.matmul(bank[STAT_BANK][:], mean_w[:], accl[:], start=False, stop=True).then_inc(stat_mm, 1)

            pe.wait_ge(const_done, 3)
            first_units(U_AX, MIX_BANKS, 0)
            for c in range(2, U_GATES):
                if c >= 4:
                    pe.wait_ge(mix_free, c - 3)
                whole(c, MIX_BANKS[c % 4])
            slot = U_GATES % RING
            pe.wait_ge(w_lo, U_GATES + 1)
            for item in range(2 * MT_A):
                m, g = item // 2, item % 2
                if g == 0:
                    pe.wait_ge(ax_lo, m + 1)
                if item == 1:
                    pe.wait_ge(rstd_done, 1)
                if item >= 4:
                    pe.wait_ge(gate_sig, item - 3)
                k = g * MT_A + m
                ins = product(bank[SIDE_BANKS[item % 4]][:], wh[:, slot, k], wl[:, slot, k],
                              mxh[:, m], mxl[:, m], True, True)
                ins.then_inc(w_used if item == 2 * MT_A - 1 else gates_mm, 1)
            pe.wait_ge(ident_done, 1)
            pe.wait_ge(gelu_v, MT_A)
            for n in range(4):
                pe.wait_ge(gate_sig, 5 + n)
                for m in range(MT_A):
                    ins = nc.tensor.transpose(bank[SIDE_BANKS[n]][:, P * m:P * m + P], vg[:, m, P * n:P * n + P],
                                              ident[:])
                ins.then_inc(tr_mm, 1)
            for c in range(U_BU, U_AG0 + 1):
                pe.wait_ge(mix_free, c - 1 - 3)
                whole(c, MIX_BANKS[(c - 1) % 4])
            slot = U_SGU % RING
            pe.wait_ge(w_lo, U_SGU + 1)
            for item in range(GROUPS):
                gp, half = item // 2, item % 2
                if item < 2:
                    pe.wait_ge(v_lo, 2 * half + 2)
                if item < 4:
                    pe.wait_ge(ln_norm, item + 1)
                else:
                    pe.wait_ge(sgu_free, item - 3)
                for n in range(2):
                    ins = product(bank[SIDE_BANKS[item % 4]][:, 256 * n:256 * n + 256],
                                  mxh[:, 2 * half + n, P * gp:P * gp + P], mxl[:, 2 * half + n, P * gp:P * gp + P],
                                  wh[:, slot, 2 * gp:2 * gp + 2].rearrange("p a b -> p (a b)"),
                                  wl[:, slot, 2 * gp:2 * gp + 2].rearrange("p a b -> p (a b)"), True, True)
                ins.then_inc(w_used if item == GROUPS - 1 else sgu_mm, 1)
            for c in range(U_AG1, U_OUT):
                pe.wait_ge(mix_free, c - 2 - 3)
                whole(c, MIX_BANKS[(c - 2) % 4])

            def residual_start(unit, banks, src, order, ready):
                for b in range(2):
                    pe.wait_ge(w_lo, unit + b + 1)
                    for n, k in enumerate(order[:-1]):
                        ready(n)
                        tiles(bank[banks[b]][:], unit + b, [k], n == 0, False, src)
                ready(KT - 1)
                for b in range(2):
                    tiles(bank[banks[b]][:], unit + b, [order[-1]], False, True, src).then_inc(w_used, 1)

            def residual_rest(unit, stage, src):
                for m in range(2, KT):
                    pe.wait_ge(x_ready, stage * KT + m - 1)
                    whole(unit + m, RES_BANKS[stage][m % 2], src=src)

            pe.wait_ge(sgu_free, GROUPS)
            residual_start(U_OUT, RES_BANKS[0], (yh, yl), Y_ORDER, lambda n: pe.wait_ge(y_lo, n + 1))
            residual_rest(U_OUT, 0, (yh, yl))

            def ffn(layer):
                base = U_UP[layer]
                if layer:
                    pe.wait_ge(x_ready, 3 * KT)
                first_units(base, UP_BANKS, 1 + 2 * layer)
                for t in range(2, 6):
                    if t == 5:
                        pe.wait_ge(rstd_done, 2 + 2 * layer)
                    whole(base + t, UP_BANKS[t])
                with pe.Fori(0, FF_PAIRS // 3 - 1) as turn:
                    for t in range(6):
                        pe.wait_ge(up_free[layer], t + 1 + 6 * turn)
                        whole(base + 6 + t, UP_BANKS[t], turn)
                pe.wait_ge(up_free[layer], 2 * FF_PAIRS - 5)
                whole(base + 2 * FF_PAIRS, UP_BANKS[0])

                stage = 1 + 2 * layer
                base = U_DOWN[layer]
                with pe.Fori(0, KT // 2) as turn:
                    for mm in range(2):
                        dst = bank[RES_BANKS[stage][mm]][:]
                        pe.wait_ge(x_ready, stage * KT + mm - 1 + 2 * turn)
                        for u in range(3):
                            unit = base + 3 * mm + u
                            slot = unit % RING
                            pe.wait_ge(w_lo, unit + 1 + RAW * turn)
                            for k in range(DOWN_KT[u]):
                                kt = 8 * u + k
                                rows = P if kt < FF_PAIRS else FF_TAIL
                                if mm == 0:
                                    pe.wait_ge(act_lo[layer], kt + 1)
                                ins = product(dst, wh[0:rows, slot, k], wl[0:rows, slot, k],
                                              ah[0:rows, kt], al[0:rows, kt], kt == 0, kt == FF_KT - 1)
                            ins.then_inc(w_used, 1)

            ffn(0)

            def transpose_v(c, turn):
                if c >= 1 or not isinstance(turn, int):
                    pe.wait_ge(ptr_lo, 7 * c - 1 + 14 * turn)
                pe.wait_ge(qkv_out, 3 * c + 3 + 6 * turn)
                for n in range(4):
                    ins = nc.tensor.transpose(bank[TR_BANKS[c % 2]][:, P * n:P * n + P], v_sb[:, P * n:P * n + P],
                                              ident[:])
                ins.then_inc(ptr_mm, 1)

            def scores(c, turn, hh):
                head = 2 * c + hh
                rows = slice(HD * hh, HD * hh + HD)
                if hh == 0:
                    pe.wait_ge(qk_lo, 2 * c + 2 + 4 * turn)
                for g, group in enumerate(SCORE_GROUPS):
                    if head >= 1 or not isinstance(turn, int):
                        pe.wait_ge(score_out, 4 * (head - 1) + (1, 3, 4)[g] + 16 * turn)
                    for i, col in group:
                        n = P * (i + 1)
                        ins = product(bank[SCORE_BANKS[g]][:, col:col + n],
                                      qh[rows, c % 2, P * i:P * i + P], ql[rows, c % 2, P * i:P * i + P],
                                      kh[rows, c % 2, 0:n], kl[rows, c % 2, 0:n], True, True)
                    ins.then_inc(score_mm, 1)

            def transpose_p(c, turn, t):
                hh, g = (t - 1) // 3, (t - 1) % 3
                if g == 0:
                    pe.wait_ge(p_norm, 4 * (2 * c + hh) + 4 + 16 * turn)
                if t >= 2 or c >= 1 or not isinstance(turn, int):
                    pe.wait_ge(ptr_lo, 7 * c + t - 1 + 14 * turn)
                for n, (i, j) in enumerate(TR_GROUPS[g]):
                    ins = nc.tensor.transpose(bank[TR_BANKS[(c + t) % 2]][:, P * n:P * n + P],
                                              p_sb[:, hh, P_OFF[i] + P * j:P_OFF[i] + P * j + P], ident[:])
                ins.then_inc(ptr_mm, 1)

            def weighted_v(c, turn, hh):
                pe.wait_ge(ptr_lo, 7 * c + 3 * hh + 4 + 14 * turn)
                if c + hh >= 1 or not isinstance(turn, int):
                    pe.wait_ge(o_lo, 2 * c + hh + 4 * turn)
                for j in range(4):
                    src = slice(KEY_OFF[j], KEY_OFF[j] + T - P * j)
                    ins = product(bank[AV_BANK][:, P * j:T], vh[:, P * j:P * j + P], vl[:, P * j:P * j + P],
                                  pth[:, hh, src], ptl[:, hh, src], j == 0, j == 3)
                ins.then_inc(av_mm, 1)

            def project(c, turn, which, ks=range(KT)):
                unit = U_QKV + 3 * c + which
                first, last = ks[0] == 0, ks[-1] == KT - 1
                if first:
                    pe.wait_ge(w_lo, unit + 1 + RAW * turn)
                    if 3 * c + which >= 2 or not isinstance(turn, int):
                        pe.wait_ge(qkv_out, 3 * c + which - 1 + 6 * turn)
                ins = tiles(bank[ATT_PROJ_BANKS[(c + which) % 2]][:], unit, ks, first, last, (xh, xl))
                if last:
                    ins.then_inc(w_used, 1)

            def attend(c, turn, fill):
                transpose_v(c, turn)
                scores(c, turn, 0)
                fill(0)
                scores(c, turn, 1)
                transpose_p(c, turn, 1)
                transpose_p(c, turn, 2)
                fill(1)
                transpose_p(c, turn, 3)
                fill(2)
                weighted_v(c, turn, 0)
                transpose_p(c, turn, 4)
                transpose_p(c, turn, 5)
                fill(3)
                transpose_p(c, turn, 6)
                fill(4)
                weighted_v(c, turn, 1)

            def next_pair(c, turn):
                parts = [(0, range(KT)), (1, range(4)), (1, range(4, KT)), (2, range(4)), (2, range(4, KT))]
                return lambda n: project(c + 1, turn, *parts[n])

            first_units(U_QKV, ATT_PROJ_BANKS, 2)
            pe.wait_ge(rstd_done, 3)
            project(0, 0, 2)
            attend(0, 0, next_pair(0, 0))
            attend(1, 0, next_pair(1, 0))
            with pe.Fori(0, PAIRS // 2 - 2) as turn:
                attend(2, turn, next_pair(2, turn))
                attend(3, turn, next_pair(3, turn))
            attend(PAIRS - 2, 0, next_pair(PAIRS - 2, 0))

            def output_part(n):
                b, ks = [(0, (0, 1, 2)), (0, (3, 4)), (0, (5, 6)), (1, (0, 1, 2, 3)), (1, (4, 5, 6))][n]
                if n in (0, 3):
                    pe.wait_ge(w_lo, U_WO + b + 1)
                    pe.wait_ge(qkv_out, 3 * PAIRS)
                if n in (0, 1, 2):
                    pe.wait_ge(o_lo, 2 * ks[-1] + 2)
                tiles(bank[RES_BANKS[2][b]][:], U_WO + b, ks, ks[0] == 0, False, (oh, ol))

            attend(PAIRS - 1, 0, output_part)
            pe.wait_ge(o_lo, HEADS)
            for b in range(2):
                tiles(bank[RES_BANKS[2][b]][:], U_WO + b, [KT - 1], False, True, (oh, ol)).then_inc(w_used, 1)
            residual_rest(U_WO, 2, (oh, ol))
            ffn(1)
            statistics(4)


LRU_STEPS = 17


def column_tiles(w):
    return w.reshape(KT, P, -1, P).transpose(2, 1, 0, 3)


def pack_weights(w_in, gate_r, gate_i, sgu_w, w_out, w_qkv, w_o, w_up, w_down):
    zin = column_tiles(w_in)
    a_x, a_g, b_u, b_v = (zin[MT_A * q:MT_A * q + MT_A] for q in range(4))
    gates = np.zeros((1, P, KT, P), w_in.dtype)
    for g, w in enumerate((gate_r, gate_i)):
        for m in range(MT_A):
            for half in range(2):
                at = slice(64 * half, 64 * half + 64)
                gates[0, at, g * MT_A + m, at] = w[2 * m + half]
    sgu = sgu_w.transpose(2, 0, 1)[None]
    parts = [a_x, b_v, gates, b_u, a_g[0:1], sgu, a_g[1:], column_tiles(w_out)]

    def up(w):
        g = column_tiles(w[:, 0:FF_PAIRS * P])
        u = column_tiles(w[:, D_FF:D_FF + FF_PAIRS * P])
        pairs = np.stack([g, u], 1).reshape(2 * FF_PAIRS, P, KT, P)
        tail = np.concatenate([w[:, FF_PAIRS * P:D_FF], w[:, D_FF + FF_PAIRS * P:]], 1)
        return [pairs, column_tiles(tail)]

    def down(w):
        full = np.concatenate([w, np.zeros((3 * D - D_FF, D), w.dtype)], 0)
        return full.reshape(3, KT, P, KT, P).transpose(3, 0, 2, 1, 4).reshape(3 * KT, P, KT, P)

    parts += up(w_up[0]) + [down(w_down[0])]
    parts.append(column_tiles(w_qkv).reshape(3, PAIRS, P, KT, P).transpose(1, 0, 2, 3, 4).reshape(-1, P, KT, P))
    parts.append(column_tiles(w_o))
    parts += up(w_up[1]) + [down(w_down[1])]
    return np.concatenate([p.reshape(-1, P, UNIT) for p in parts], 0)


def pack_params(norms, conv_w, conv_b, lru_conv_w, lru_conv_b, r_b, i_b, lam):
    cols = [n.reshape(KT, P).T for n in norms]
    for layer in range(2):
        rows = np.concatenate([conv_w[layer], conv_b[layer][None]], 0)
        g, u = rows[:, 0:D_FF], rows[:, D_FF:]
        full = np.stack([v[:, 0:FF_PAIRS * P].reshape(4, FF_PAIRS, P) for v in (g, u)])
        cols.append(full.transpose(3, 2, 0, 1).reshape(P, 8 * FF_PAIRS))
        tail = np.concatenate([g[:, FF_PAIRS * P:], u[:, FF_PAIRS * P:]], 1).T
        cols += [tail, np.zeros((P, 4), tail.dtype)]
    lru = np.concatenate([lru_conv_w, lru_conv_b[None], r_b[None], i_b[None], lam[None]], 0)
    cols.append(lru.reshape(8, MT_A, P).transpose(2, 1, 0).reshape(P, 8 * MT_A))
    return np.concatenate(cols, 1)


def kernel(**inputs):
    import concourse.bacc as bacc
    from concourse.bass_utils import run_bass_kernel_spmd

    a = {k: np.asarray(v) for k, v in inputs.items()}
    arrays = {
        "x_in": a["x"][0].T.reshape(KT, P, T).transpose(1, 0, 2),
        "weights": pack_weights(a["w_in_ab"][0], a["lru_gate_r_w"][0], a["lru_gate_i_w"][0], a["sgu_w"][0],
                                a["w_out_ab"][0], a["w_qkv"][0], a["w_o"][0], a["ffn_w_up"], a["ffn_w_down"]),
        "params": pack_params([a["norm_ab"][0], a["norm_ffn"][0], a["norm_attn"][0], a["norm_ffn"][1],
                               a["norm_final"]], a["ffn_conv_w"], a["ffn_conv_b"], a["lru_conv_w"][0],
                              a["lru_conv_b"][0], a["lru_gate_r_b"][0], a["lru_gate_i_b"][0], a["lru_lambda"][0]),
        "rel_rev": a["rel_bias"][0][:, ::-1],
        "ln_g": a["sgu_ln_g"],
        "ln_b": a["sgu_ln_b"],
        "sgu_b": a["sgu_b"][0],
    }
    arrays = {k: np.ascontiguousarray(v) for k, v in arrays.items()}
    nc = bacc.Bacc("TRN2", target_bir_lowering=False, num_devices=1)
    args = [nc.dram_tensor(n, v.shape, mybir.dt.from_np(v.dtype), kind="ExternalInput").ap()
            for n, v in arrays.items()]
    out = nc.dram_tensor("out", (P, KT, T), F32, kind="ExternalOutput").ap()
    trunk(nc, *args, out)
    got = run_bass_kernel_spmd(nc, [arrays], core_ids=[0]).results[0]["out"]
    return got.transpose(1, 0, 2).reshape(D, T).T[None]
```

```python
from contextlib import ExitStack

import numpy as np

import concourse.bass as bass
from concourse import mybir

F32 = mybir.dt.float32
F32R = mybir.dt.float32r
ACT = mybir.ActivationFunctionType
ALU = mybir.AluOpType

P = 128
D = 1024
T = 512
KT = D // P
CHUNK = 64
HEADS, HD = 16, 64
PAIRS = HEADS // 2
MAX_REL = 256
D_A = 512
MT_A = D_A // P
A_CONV = 4
GROUPS = 8
D_FF = 2752
FF_PAIRS = D_FF // P
FF_TAIL = D_FF - FF_PAIRS * P
FF_KT = FF_PAIRS + 1
EPS = 1e-6
MASKED = 1e30

RAW = 6
RING = 3
UNIT = KT * P
LAG = 5
FIRST = UNIT // 2

WARM_UP = 14

U_AX, U_BV, U_GATES, U_BU, U_AG0, U_SGU, U_AG1 = 0, 4, 8, 9, 13, 14, 15
U_OUT = 18
U_UP = [U_OUT + KT, 0]
U_DOWN = [U_UP[0] + 2 * FF_PAIRS + 1, 0]
U_QKV = U_DOWN[0] + 3 * KT
U_WO = U_QKV + 3 * PAIRS
U_UP[1] = U_WO + KT
U_DOWN[1] = U_UP[1] + 2 * FF_PAIRS + 1
UNITS = U_DOWN[1] + 3 * KT

N_NORMS = 5
C_GAIN = 0
HALF = T // 2
OUT_POOL = 3
C_FFN = C_GAIN + N_NORMS * KT
FFN_COLS = FF_KT * 8
C_LRU = C_FFN + 2 * FFN_COLS
N_PARAMS = C_LRU + MT_A * 8

EXT = T + P
EXT_CLIP = T - MAX_REL - 1

STAT_BANK = 7
MIX_BANKS = [0, 1, 2, 5]
SIDE_BANKS = [6, 7, 3, 4]
UP_BANKS = [0, 1, 2, 5, 6, 7]
CONV_BANKS = [3, 4]
ATT_PROJ_BANKS = [0, 1]
SCORE_BANKS = [[2, 3], [4, 5], [2, 3]]
FINAL_BANKS = [4, 5]
FINAL_STAT_BANKS = [7, 6]
TR_BANKS = [7, 6]
AV_BANK = 5
RES_BANKS = [[3, 4] * 4, [3, 4] * 4, [0, 1] + [3, 4] * 3, [3, 4] * 4]

Y_ORDER = [4, 5, 6, 7, 0, 1, 2, 3]

SCORE_GROUPS = [[(3, 0)], [(2, 0), (0, 384)], [(1, 0)]]
SCORE_STEPS = [(hh, i) for group in SCORE_GROUPS for hh in range(2) for i, _ in group]
P_OFF = [0, 128, 384, 768]
P_COLS = 1280
TR_GROUPS = [[(0, 0), (1, 0), (2, 0), (3, 0)], [(1, 1), (2, 1), (3, 1), (3, 3)], [(2, 2), (3, 2)]]
TR_OFF = [0, 512, 1024]
KEY_OFF = [0, 512, 1024, 896]


class Steps:

    def __init__(self, sem):
        self.sem, self.n, self.turn, self.per = sem, 0, None, 0

    def enter(self, turn, per):
        self.turn, self.per, self.at = turn, per, self.n

    def leave(self, turns):
        assert self.n - self.at == self.per, (self.n - self.at, self.per)
        self.n, self.turn = self.at + turns * self.per, None

    def value(self):
        return self.n if self.turn is None else self.turn * self.per + self.n


def trunk(nc, x_in, weights, params, rel_rev, ln_g, ln_b, sgu_b, out):
    ctx = ExitStack()
    with ctx:
        def persistent(name, shape, dt):
            return ctx.enter_context(nc.sbuf_tensor(name, shape, dt))

        def sem(name):
            return ctx.enter_context(nc.semaphore(name))

        x = persistent("x", [P, KT, T], F32)
        xh = persistent("xh", [P, KT, T], F32R)
        xl = persistent("xl", [P, KT, T], F32R)
        raw = persistent("raw", [P, RAW, UNIT], F32)
        wh = persistent("wh", [P, RING, KT, P], F32R)
        wl = persistent("wl", [P, RING, KT, P], F32R)
        par = persistent("par", [P, N_PARAMS], F32)
        ident = persistent("ident", [P, P], F32)
        rstd = persistent("rstd", [P, T], F32)
        acc = persistent("acc", [P, T], F32)
        sq = persistent("sq", [P, 2, T], F32)
        small = persistent("small", [P, 62], F32)
        eps = small[:, 0:1]
        idle = small[:, 1:2]
        neg_min = small[:, 2:10]
        psums = small[:, 10:18]
        lru_rate = small[:, 18:22]
        ln_mv = small[:, 22:30].rearrange("p (n c) -> p n c", c=2)
        ln_var = small[:, 30:34]
        ln_rstd = small[:, 34:38]
        ln_tmp = small[:, 38:42]
        idle2 = small[:, 42:43]
        gate_word = small[:, 43:49]
        mean_w = small[:, 49:50]
        root = small[:, 50:54]
        rstd_col = small[:, 54:58]
        newt = small[:, 58:62]
        bn6 = persistent("bn6", [P, 4, 6], F32)

        with ExitStack() as phase:
            def mixer(name, shape, dt):
                return phase.enter_context(nc.sbuf_tensor(name, shape, dt))

            base_y = nc.sbuf_base
            yh = mixer("yh", [P, KT, T], F32R)
            yl = mixer("yl", [P, KT, T], F32R)
            decay = nc.alloc_sbuf_tensor_at("decay", [P, MT_A, T], F32, offset=base_y)
            expm = nc.alloc_sbuf_tensor_at("expm", [P, MT_A, T], F32, offset=base_y + KT * T * 4)
            mxh = mixer("mxh", [P, MT_A, T], F32R)
            mxl = mixer("mxl", [P, MT_A, T], F32R)
            axc = mixer("axc", [P, MT_A, T], F32)
            rec = mixer("rec", [P, MT_A, T], F32)
            vg = mixer("vg", [P, MT_A, T], F32)
            gu = mixer("gu", [P, MT_A, T], F32)
            lng = mixer("lng", [P, D_A], F32)
            lnb = mixer("lnb", [P, D_A], F32)
            sgb = mixer("sgb", [P, GROUPS // 2, P], F32)
            axp = mixer("axp", [P, A_CONV - 1 + T], F32)
            maskt = mixer("maskt", [CHUNK, HEADS, CHUNK], F32)
            relt = mixer("relt", [HEADS, 2 * MAX_REL + 1], F32)
            ext = mixer("ext", [HEADS, EXT], F32)

        with ExitStack() as phase:
            def ffn_mem(name, shape, dt):
                return phase.enter_context(nc.sbuf_tensor(name, shape, dt))

            ah = ffn_mem("ah", [P, FF_KT, T], F32R)
            al = ffn_mem("al", [P, FF_PAIRS, T], F32R)
            ub = [ffn_mem(f"ub{i}", [P, 2 + T], F32) for i in range(2)]
            cg = ffn_mem("cg", [P, T], F32)
            cu = ffn_mem("cu", [P, T], F32)

        with ExitStack() as phase:
            def att_mem(name, shape, dt):
                return phase.enter_context(nc.sbuf_tensor(name, shape, dt))

            oh = att_mem("oh", [P, PAIRS, T], F32R)
            ol = att_mem("ol", [P, PAIRS, T], F32R)
            qh = att_mem("qh", [P, T], F32R)
            ql = att_mem("ql", [P, T], F32R)
            kh = att_mem("kh", [P, T], F32R)
            kl = att_mem("kl", [P, T], F32R)
            vv = att_mem("vv", [P, 4, 2, P], F32R)
            pth = att_mem("pth", [P, 2, P_COLS], F32R)
            ptl = att_mem("ptl", [P, 2, P_COLS], F32R)
            p_sb = att_mem("p_sb", [P, 2, P_COLS], F32)
            q_sb = att_mem("q_sb", [P, T], F32)
            k_sb = att_mem("k_sb", [P, T], F32)
            v_sb = att_mem("v_sb", [P, T], F32)
            o_sb = att_mem("o_sb", [P, T], F32)
            bias = att_mem("bias", [P, 2, 2, T], F32)

        bank = [ctx.enter_context(nc.psum_tensor(f"bank{i}", [P, T], F32)) for i in range(8)]

        ext_d = nc.dram_tensor("ext_scratch", (HEADS, EXT), F32).ap()
        bias_d = nc.dram_tensor("bias_scratch", (HEADS, P, T), F32).ap()

        raw_in = [sem(f"raw_in{i}") for i in range(RAW)]
        x_in_sem = [sem(f"x_in{i}") for i in range(KT)]
        first_in, first_hi, first_lo, warm_ready = (sem(n) for n in ("first_in", "first_hi", "first_lo", "warm_ready"))
        gains_in, rate_done = sem("gains_in"), sem("rate_done")
        par_in, rel_in, ext_out, bias_out = sem("par_in"), sem("rel_in"), sem("ext_out"), sem("bias_out")
        mask_out, ln_in, out_done = sem("mask_out"), sem("ln_in"), sem("out_done")
        bias_in = [sem(f"bias_in{i}") for i in range(2)]
        w_hi, w_lo, w_used = sem("w_hi"), sem("w_lo"), sem("w_used")
        x_ready, x_hi, x_lo, x_sq, x_acc = (sem(n) for n in ("x_ready", "x_hi", "x_lo", "x_sq", "x_acc"))
        stat_mm, root_done, col_done, spread_mm, rstd_done = (
            sem(n) for n in ("stat_mm", "root_done", "col_done", "spread_mm", "rstd_done"))
        dve_step, pool_step = sem("dve_step"), sem("pool_step")
        const_done, ident_done, maskt_done, ext_done = (
            sem(n) for n in ("const_done", "ident_done", "maskt_done", "ext_done"))
        lam_abs, lam_exp, mix_free, ax_conv, ax_hi, ax_lo, gelu_v = (
            sem(n) for n in ("lam_abs", "lam_exp", "mix_free", "ax_conv", "ax_hi", "ax_lo", "gelu_v"))
        gates_mm, gate_sig, ix_done, tanh_done, expm_done, expm_root = (
            sem(n) for n in ("gates_mm", "gate_sig", "ix_done", "tanh_done", "expm_done", "expm_root"))
        tr_mm, ln_var_done, ln_root, ln_norm, ln_affine, v_hi, v_lo = (
            sem(n) for n in ("tr_mm", "ln_var_done", "ln_root", "ln_norm", "ln_affine", "v_hi", "v_lo"))
        sgu_masked, sgu_mm, sgu_free, gelu_u, gelu_g, y_prod, y_hi, y_lo = (
            sem(n) for n in ("sgu_masked", "sgu_mm", "sgu_free", "gelu_u", "gelu_g", "y_prod", "y_hi", "y_lo"))
        up_free, conv_done, silu_done, prod_done, act_hi, act_lo = (
            [sem(f"{n}{layer}") for layer in range(2)]
            for n in ("up_free", "conv_done", "silu_done", "prod_done", "act_hi", "act_lo"))
        qkv_out, qk_hi, qk_lo, score_mm, score_out, exp_done, p_norm = (
            sem(n) for n in ("qkv_out", "qk_hi", "qk_lo", "score_mm", "score_out", "exp_done", "p_norm"))
        ptr_mm, ptr_hi, ptr_lo, av_mm, o_half, o_sum, o_hi, o_lo, rsum_inv = (
            sem(n) for n in ("ptr_mm", "ptr_hi", "ptr_lo", "av_mm", "o_half", "o_sum", "o_hi", "o_lo", "rsum_inv"))
        final_mm, x_last, final_sq, out_dve, out_pool = (
            sem(n) for n in ("final_mm", "x_last", "final_sq", "out_dve", "out_pool"))

        def gain(norm, m):
            return par[:, bass.ds(m + (C_GAIN + norm * KT), 1)] if not isinstance(m, int) \
                else par[:, C_GAIN + norm * KT + m:C_GAIN + norm * KT + m + 1]

        def lru_par(m, k):
            return par[:, C_LRU + 8 * m + k:C_LRU + 8 * m + k + 1]

        def tile_of(buf, m):
            return buf[:, m] if isinstance(m, int) else buf[:, bass.ds(m, 1), :]

        def proj_bank(c, turn, which):
            if (c, turn, which) == (0, 0, 2):
                return AV_BANK
            return ATT_PROJ_BANKS[(c + which) % 2]

        block = ctx.enter_context(nc.Block())

        @block.sync
        def _(sp):
            def load_unit(c, turn=0):
                n = c + RAW * turn
                if c >= RAW or not isinstance(turn, int):
                    sp.wait_ge(w_lo, n - (RAW - 1))
                at = weights[n] if isinstance(n, int) else weights[bass.ds(n, 1)].rearrange("u p c -> (u p) c")
                sp.dma_start(raw[:, c % RAW, :], at).then_inc(raw_in[c % RAW], 16)

            sp.dma_start(par[:, 0:C_FFN], params[:, 0:C_FFN]).then_inc(gains_in, 16)
            sp.dma_start(raw[:, 0, 0:FIRST], weights[0, :, 0:FIRST]).then_inc(first_in, 16)
            sp.dma_start(x[:, 0], x_in[:, 0]).then_inc(x_in_sem[0], 16)
            sp.dma_start(raw[:, 0, FIRST:], weights[0, :, FIRST:]).then_inc(raw_in[0], 16)
            for m in range(1, KT):
                sp.dma_start(x[:, m], x_in[:, m]).then_inc(x_in_sem[m], 16)
                if m in (5, 7):
                    load_unit(m // 2 - 1)
            sp.dma_start(par[:, C_FFN:], params[:, C_FFN:]).then_inc(par_in, 16)
            for c in range(3, RAW):
                load_unit(c)
            sp.dma_start(relt[:], rel_rev).then_inc(rel_in, 16)
            sp.dma_start(lng[:], bass.AP(ln_g.tensor, 0, [[0, P], [1, D_A]])).then_inc(ln_in, 16)
            sp.dma_start(lnb[:], bass.AP(ln_b.tensor, 0, [[0, P], [1, D_A]])).then_inc(ln_in, 16)
            for half in range(2):
                sp.dma_start(sgb[half * 64:half * 64 + 64],
                             bass.AP(sgu_b.tensor, half * P, [[0, 64], [2 * P, GROUPS // 2], [1, P]])
                             ).then_inc(ln_in, 16)
            for c in range(RAW, 2 * RAW):
                load_unit(c)
            sp.wait_ge(ext_done, 1)
            sp.dma_start(ext_d, ext[:]).then_inc(ext_out, 16)
            load_unit(2 * RAW)
            load_unit(2 * RAW + 1)
            sp.wait_ge(ext_out, 16)
            sp.dma_start(bias_d, bass.AP(ext_d.tensor, P - 1, [[EXT, HEADS], [-1, P], [1, T]])).then_inc(bias_out, 16)
            for c in range(2 * RAW + 2, 3 * RAW):
                load_unit(c)
            sp.wait_ge(bias_out, 16)
            sp.wait_ge(maskt_done, 1)
            sp.dma_start(bias_d[:, 0:CHUNK, T - CHUNK:T].rearrange("h p c -> p h c"), maskt[:]).then_inc(mask_out, 16)
            with sp.Fori(0, UNITS // RAW - 3) as turn:
                for c in range(3 * RAW, 4 * RAW):
                    load_unit(c, turn)
            for half in range(2):
                cols = slice(HALF * half, HALF * half + HALF)
                sp.wait_ge(out_dve, (KT - OUT_POOL) * half + 2)
                sp.dma_start(out[:, OUT_POOL:OUT_POOL + 2, cols], x[:, OUT_POOL:OUT_POOL + 2, cols]).then_inc(out_done, 16)
                sp.wait_ge(out_dve, (KT - OUT_POOL) * (half + 1))
                sp.dma_start(out[:, OUT_POOL + 2:, cols], x[:, OUT_POOL + 2:, cols]).then_inc(out_done, 16)
                sp.wait_ge(out_pool, OUT_POOL * (half + 1))
                sp.dma_start(out[:, 0:OUT_POOL, cols], x[:, 0:OUT_POOL, cols]).then_inc(out_done, 16)
            sp.wait_ge(out_done, 16 * 6)

        @block.gpsimd
        def _(pool):
            steps = Steps(pool_step)

            def link(ins):
                ins.then_inc(pool_step, 1)
                steps.n += 1
                pool.wait_ge(pool_step, steps.value())

            def split_lo(c, turn=0):
                pool.wait_ge(w_hi, c + 1 + RAW * turn)
                nc.gpsimd.tensor_tensor(
                    wl[:, c % RING].rearrange("p k c -> p (k c)"), raw[:, c % RAW],
                    wh[:, c % RING].rearrange("p k c -> p (k c)"), ALU.subtract).then_inc(w_lo, 1)

            nc.gpsimd.memset(eps, EPS).then_inc(const_done, 1)
            nc.gpsimd.memset(idle, 0.0).then_inc(const_done, 1)
            nc.gpsimd.memset(mean_w, 1.0 / D).then_inc(const_done, 1)
            link(nc.gpsimd.memset(ident[:], 0.0))
            nc.gpsimd.affine_select(out=ident[:], in_=ident[:], compare_op=ALU.not_equal, fill=1.0, base=0,
                                    pattern=[[-1, P]], channel_multiplier=1).then_inc(ident_done, 1)
            w0h, w0l = (w[:, 0].rearrange("p k c -> p (k c)") for w in (wh, wl))
            pool.wait_ge(first_hi, 1)
            nc.gpsimd.tensor_tensor(w0l[:, 0:FIRST], raw[:, 0, 0:FIRST], w0h[:, 0:FIRST], ALU.subtract
                                    ).then_inc(first_lo, 1)
            pool.wait_ge(w_hi, 1)
            nc.gpsimd.tensor_tensor(w0l[:, FIRST:], raw[:, 0, FIRST:], w0h[:, FIRST:], ALU.subtract).then_inc(w_lo, 1)
            split_lo(1)
            split_lo(2)
            nc.gpsimd.memset(maskt[:], MASKED).then_inc(maskt_done, 1)
            for c in range(3, U_AG0):
                split_lo(c)
            pool.wait_ge(raw_in[U_SGU % RAW], 16 * (U_SGU // RAW + 1))
            pool.wait_ge(w_lo, U_AG0)
            nc.gpsimd.memset(raw[CHUNK:P, U_SGU % RAW].rearrange("p (g i) -> p g i", g=GROUPS)[:, :, 0:CHUNK],
                             0.0).then_inc(sgu_masked, 1)
            pool.wait_ge(sgu_masked, 1)
            split_lo(U_AG0)
            for c in range(U_SGU, 3 * RAW):
                split_lo(c)
            with pool.Fori(0, UNITS // RAW - 3) as turn:
                for c in range(3 * RAW, 4 * RAW):
                    split_lo(c, turn)
            pool.wait_ge(x_hi, 5 * KT - 1)
            for half in range(2):
                pool.wait_ge(rstd_done, 5 + half)
                cols = slice(HALF * half, HALF * half + HALF)
                for m in range(OUT_POOL):
                    nc.gpsimd.tensor_tensor(x[:, m, cols], x[:, m, cols], rstd[:, cols], ALU.mult).then_inc(out_pool, 1)

        @block.scalar
        def _(act):
            def split_hi(c, turn=0):
                if c >= UNITS:
                    return
                act.wait_ge(raw_in[c % RAW], 16 * (c // RAW + 1) + 16 * turn)
                if c == U_SGU:
                    act.wait_ge(sgu_masked, 1)
                if c >= RING:
                    act.wait_ge(w_used, c - (RING - 1) + RAW * turn)
                nc.scalar.activation(wh[:, c % RING].rearrange("p k c -> p (k c)"), raw[:, c % RAW],
                                     ACT.Copy).then_inc(w_hi, 1)

            def norm_hi(norm, m):
                nc.scalar.activation(tile_of(xh, m), tile_of(x, m), ACT.Copy, scale=gain(norm, m)).then_inc(x_hi, 1)

            def square_free(norm, m):
                act.wait_ge(x_acc, norm * KT + m - 1)

            def norm_square(norm, m, even):
                xm = tile_of(x, m)
                nc.scalar.activation(tile_of(sq, even) if isinstance(m, int) else sq[:, even:even + 1, :],
                                     xm, ACT.Square).then_inc(x_sq, 1)

            def norm_tile(norm, m, even):
                xm = tile_of(x, m)
                square_free(norm, m)
                if norm < 4:
                    norm_hi(norm, m)
                norm_square(norm, m, even)
                if norm == 4:
                    nc.scalar.activation(xm, xm, ACT.Copy, scale=gain(norm, m)).then_inc(x_hi, 1)

            def statistics(norm):
                act.wait_ge(stat_mm, norm + 1)
                nc.scalar.activation(root, bank[STAT_BANK][:, 0:4], ACT.Sqrt, bias=eps).then_inc(root_done, 1)
                act.wait_ge(spread_mm, norm + 1)
                nc.scalar.activation(rstd[:], bank[STAT_BANK][:], ACT.Copy).then_inc(rstd_done, 1)

            def preload(func):
                nc.scalar.activation(idle2, idle, func)

            w0h = wh[:, 0].rearrange("p k c -> p (k c)")
            act.wait_ge(const_done, 3)
            act.wait_ge(first_in, 16)
            nc.scalar.activation(w0h[:, 0:FIRST], raw[:, 0, 0:FIRST], ACT.Copy).then_inc(first_hi, 1)
            act.wait_ge(gains_in, 16)
            for m in range(KT + LAG):
                if m < KT:
                    act.wait_ge(x_in_sem[m], 16)
                    norm_hi(0, m)
                if m == 0:
                    act.wait_ge(raw_in[0], 16)
                    nc.scalar.activation(w0h[:, FIRST:], raw[:, 0, FIRST:], ACT.Copy).then_inc(w_hi, 1)
                if m in (5, 7):
                    split_hi(m // 2 - 1)
                if m >= LAG:
                    if m >= LAG + 2:
                        square_free(0, m - LAG)
                    norm_square(0, m - LAG, (m - LAG) % 2)
            act.wait_ge(lam_abs, 1)
            nc.scalar.activation(ln_tmp, ln_var, ACT.Exp, scale=-1.0).then_inc(lam_exp, 1)
            split_hi(U_AX + 3)
            statistics(0)
            for m in range(MT_A):
                split_hi(U_AX + m + 4)
                act.wait_ge(ax_conv, m + 1)
                nc.scalar.activation(mxh[:, m], axc[:, m], ACT.Copy).then_inc(ax_hi, 1)
            for m in range(MT_A):
                if m < MT_A - 1:
                    split_hi(U_BV + m + 4)
                act.wait_ge(mix_free, MT_A + m + 1)
                nc.scalar.activation(vg[:, m], vg[:, m], ACT.Gelu_apprx_tanh).then_inc(gelu_v, 1)
            for item in range(2 * MT_A):
                m = item // 2
                if item < 2 * MT_A - 1:
                    act.wait_ge(gates_mm, item + 1)
                else:
                    act.wait_ge(w_used, U_GATES + 1)
                nc.scalar.activation((expm if item % 2 else rec)[:, m], bank[SIDE_BANKS[item % 4]][:],
                                     ACT.Sigmoid, bias=lru_par(m, 5 + item % 2)).then_inc(gate_sig, 1)
            split_hi(U_GATES + 3)
            act.wait_ge(gate_sig, 2 * MT_A)
            act.wait_ge(rate_done, 1)
            for m in range(MT_A):
                nc.scalar.activation(decay[:, m], rec[:, m], ACT.Exp, scale=lru_rate[:, m:m + 1])
                act.wait_ge(ix_done, m + 1)
                nc.scalar.activation(expm[:, m], rec[:, m], ACT.Tanh, scale=lru_rate[:, m:m + 1]).then_inc(tanh_done, 1)
            split_hi(U_BU + 3)
            for m in range(MT_A):
                act.wait_ge(expm_done, m + 1)
                nc.scalar.activation(expm[:, m], expm[:, m], ACT.Sqrt, scale=-1.0).then_inc(expm_root, 1)
            act.wait_ge(ln_var_done, 1)
            nc.scalar.activation(ln_rstd, ln_var, ACT.Sqrt).then_inc(ln_root, 1)
            split_hi(U_BU + 4)
            for n in range(4):
                act.wait_ge(ln_affine, n + 1)
                nc.scalar.activation(mxh[:, n], vg[:, n], ACT.Copy).then_inc(v_hi, 1)
                if n == 1:
                    split_hi(U_BU + 5)
            preload(ACT.Gelu_apprx_tanh)
            split_hi(U_BU + 6)
            for m in range(MT_A):
                act.wait_ge(mix_free, 2 * MT_A + m + 1)
                nc.scalar.activation(gu[:, m], gu[:, m], ACT.Gelu_apprx_tanh).then_inc(gelu_u, 1)

            def gelu_gate(m):
                act.wait_ge(mix_free, 3 * MT_A + m + 1)
                nc.scalar.activation(axp[:, 0:T], axp[:, 0:T], ACT.Gelu_apprx_tanh).then_inc(gelu_g, 1)

            def split_y(s):
                act.wait_ge(y_prod, s + 1)
                src = rec if Y_ORDER[s] < MT_A else vg
                nc.scalar.activation(yh[:, Y_ORDER[s]], src[:, Y_ORDER[s] % MT_A], ACT.Copy).then_inc(y_hi, 1)

            split_hi(U_AG0 + 3)
            for s in range(4):
                split_y(s)
            split_hi(U_SGU + 3)
            gelu_gate(0)
            split_y(4)
            for m in range(1, MT_A):
                split_hi(U_AG1 + m - 1 + 3)
                gelu_gate(m)
                split_y(4 + m)

            def residual_tiles(first_unit, stage):
                for m in range(KT):
                    split_hi(first_unit + m + 3)
                    act.wait_ge(x_ready, stage * KT + m + 1)
                    norm_tile(stage + 1, m, m % 2)
                statistics(stage + 1)

            def ffn(layer):
                preload(ACT.Silu)
                base = U_UP[layer]

                def gate_up(j, turn):
                    split_hi(base + 2 * j + 3, turn)
                    split_hi(base + 2 * j + 4, turn)
                    act.wait_ge(conv_done[layer], 2 * j + 1 + RAW * turn)
                    nc.scalar.activation(cg[:], bank[CONV_BANKS[0]][:], ACT.Silu).then_inc(silu_done[layer], 1)
                    act.wait_ge(prod_done[layer], j + 1 + 3 * turn)
                    nc.scalar.activation(tile_of(ah, j + 3 * turn),
                                         bank[CONV_BANKS[1]][:].rearrange("p (a t) -> p a t", a=1),
                                         ACT.Copy).then_inc(act_hi[layer], 1)

                with act.Fori(0, FF_PAIRS // 3) as turn:
                    for j in range(3):
                        gate_up(j, turn)
                split_hi(base + 2 * FF_PAIRS + 3)
                act.wait_ge(conv_done[layer], 2 * FF_PAIRS + 1)
                nc.scalar.activation(cg[0:FF_TAIL], cg[0:FF_TAIL], ACT.Silu).then_inc(silu_done[layer], 1)
                act.wait_ge(prod_done[layer], FF_KT)
                nc.scalar.activation(ah[0:FF_TAIL, FF_PAIRS], cu[0:FF_TAIL], ACT.Copy).then_inc(act_hi[layer], 1)

                base = U_DOWN[layer]
                stage = 1 + 2 * layer

                def down(mm, turn):
                    for u in range(3):
                        split_hi(base + 3 * mm + u + 3, turn)
                    act.wait_ge(x_ready, stage * KT + mm + 1 + 2 * turn)
                    norm_tile(stage + 1, mm + 2 * turn, mm)

                with act.Fori(0, KT // 2 - 1) as turn:
                    for mm in range(2):
                        down(mm, turn)
                down(0, KT // 2 - 1)
                if layer == 0:
                    down(1, KT // 2 - 1)
                    statistics(stage + 1)

            residual_tiles(U_OUT, 0)
            ffn(0)

            preload(ACT.Exp)
            act.wait_ge(mask_out, 16)

            def load_bias(c, turn=0):
                pair2 = 2 * c + 4 * turn
                if c >= 2:
                    act.wait_ge(score_out, 8 * (c - 1) + 16 * turn)
                src = bias_d[pair2:pair2 + 2] if isinstance(turn, int) else bias_d[bass.ds(pair2, 2)]
                act.dma_start(bias[:, c % 2], src.rearrange("h p t -> p h t")).then_inc(bias_in[c % 2], 16)

            def split_qk(c, turn, which):
                act.wait_ge(qkv_out, 3 * c + which + 1 + 6 * turn)
                nc.scalar.activation((kh if which else qh)[:], (k_sb if which else q_sb)[:],
                                     ACT.Copy).then_inc(qk_hi, 1)

            def exponentials(c, turn):
                for s, (hh, i) in enumerate(SCORE_STEPS):
                    act.wait_ge(score_out, 8 * c + s + 1 + 16 * turn)
                    blk = p_sb[:, hh, P_OFF[i]:P_OFF[i] + P * (i + 1)]
                    nc.scalar.activation(blk, blk, ACT.Exp, scale=-1.0, bias=neg_min[:, 4 * hh + i:4 * hh + i + 1],
                                         accum_out=psums[:, 4 * hh + i:4 * hh + i + 1]).then_inc(exp_done, 1)

            def split_transposed(c, turn, t):
                act.wait_ge(ptr_mm, 7 * c + t + 1 + 14 * turn)
                src = bank[TR_BANKS[(c + t) % 2]]
                if t == 0:
                    nc.scalar.activation(vv[:, :, :, 0:HD], src[:].rearrange("p (j h d) -> p j h d", j=4, h=2),
                                         ACT.Copy).then_inc(ptr_hi, 1)
                    return
                hh, g = (t - 1) // 3, (t - 1) % 3
                if g == 0 and (c >= 1 or not isinstance(turn, int)):
                    act.wait_ge(av_mm, 2 * c + hh - 1 + 4 * turn)
                n = P * len(TR_GROUPS[g])
                nc.scalar.activation(pth[:, hh, TR_OFF[g]:TR_OFF[g] + n], src[:, 0:n], ACT.Copy).then_inc(ptr_hi, 1)

            def half_o(c, turn, hh):
                act.wait_ge(av_mm, 2 * c + hh + 1 + 4 * turn)
                if c >= 1 or not isinstance(turn, int):
                    act.wait_ge(o_lo, 2 * c + hh - 1 + 4 * turn)
                half, other = slice(HD * hh, HD * hh + HD), slice(HD * (1 - hh), HD * (1 - hh) + HD)
                nc.scalar.activation(o_sb[half], bank[AV_BANK][other, :], ACT.Copy).then_inc(o_half, 1)

            def split_o(c, turn, hh):
                act.wait_ge(o_sum, 2 * c + hh + 1 + 4 * turn)
                half = slice(HD * hh, HD * hh + HD)
                pair = c + 2 * turn
                dst = oh[half, pair] if isinstance(turn, int) else oh[half, bass.ds(pair, 1), :]
                src = o_sb[half, :]
                nc.scalar.activation(dst, src if isinstance(turn, int) else src.rearrange("p (a t) -> p a t", a=1),
                                     ACT.Copy).then_inc(o_hi, 1)

            def attend(c, turn, following):
                unit = U_QKV + 3 * (c + 1)
                if following:
                    load_bias(c + 1, turn)
                split_transposed(c, turn, 0)
                exponentials(c, turn)
                if following:
                    split_hi(unit + 3, turn)
                    split_qk(c + 1, turn, 0)
                for t in (1, 2, 3):
                    split_transposed(c, turn, t)
                if following:
                    split_hi(unit + 4, turn)
                    split_qk(c + 1, turn, 1)
                split_transposed(c, turn, 4)
                half_o(c, turn, 0)
                split_transposed(c, turn, 5)
                split_o(c, turn, 0)
                split_transposed(c, turn, 6)
                if following:
                    split_hi(unit + 5, turn)
                half_o(c, turn, 1)
                split_o(c, turn, 1)

            load_bias(0)
            split_hi(U_QKV + 3)
            split_qk(0, 0, 0)
            split_hi(U_QKV + 4)
            split_qk(0, 0, 1)
            split_hi(U_QKV + 5)
            attend(0, 0, True)
            attend(1, 0, True)
            with act.Fori(0, PAIRS // 2 - 2) as turn:
                attend(2, turn, True)
                attend(3, turn, True)
            attend(PAIRS - 2, 0, True)
            attend(PAIRS - 1, 0, False)
            residual_tiles(U_WO, 2)
            ffn(1)

            preload(ACT.Sqrt)
            act.wait_ge(x_acc, 5 * KT - 2)
            for half in range(2):
                cols, col2 = slice(HALF * half, HALF * half + HALF), slice(2 * half, 2 * half + 2)
                act.wait_ge(x_last, half + 1)
                nc.scalar.activation(sq[:, 1, cols], x[:, KT - 1, cols], ACT.Square).then_inc(final_sq, 1)
                act.wait_ge(stat_mm, 5 + half)
                stat = bank[FINAL_STAT_BANKS[half]]
                nc.scalar.activation(root[:, col2], stat[:, 0:2], ACT.Sqrt, bias=eps).then_inc(root_done, 1)
                act.wait_ge(spread_mm, 5 + half)
                nc.scalar.activation(rstd[:, cols], stat[:, 0:HALF], ACT.Copy).then_inc(rstd_done, 1)

        @block.vector
        def _(dve):
            steps = Steps(dve_step)

            def link(ins):
                ins.then_inc(dve_step, 1)
                steps.n += 1
                dve.wait_ge(dve_step, steps.value())

            stt = nc.vector.scalar_tensor_tensor
            tt = nc.vector.tensor_tensor
            ts = nc.vector.tensor_scalar

            def norm_lo(norm, m):
                dve.wait_ge(x_hi, norm * KT + m + 1)
                stt(tile_of(xl, m), tile_of(x, m), gain(norm, m), tile_of(xh, m),
                    ALU.mult, ALU.subtract).then_inc(x_lo, 1)

            def norm_add(norm, m, even):
                dve.wait_ge(x_sq, norm * KT + m + 1)
                if norm or m:
                    dve.wait_ge(x_acc, norm * KT + m)
                tt(acc[:], acc[:], sq[:, even], ALU.add).then_inc(x_acc, 1)

            def norm_tile(norm, m, even):
                if norm < 4:
                    norm_lo(norm, m)
                norm_add(norm, m, even)

            def inverse_root(stat, at):
                r, t = rstd_col[:, at], newt[:, at]
                link(nc.vector.reciprocal(r, root[:, at]))
                link(tt(t, r, r, ALU.mult))
                link(stt(t, stat, EPS, t, ALU.add, ALU.mult))
                link(ts(t, t, -0.5, 1.5, ALU.mult, ALU.add))
                tt(r, r, t, ALU.mult).then_inc(col_done, 1)

            def statistics(norm):
                dve.wait_ge(root_done, norm + 1)
                inverse_root(bank[STAT_BANK][:, 0:4], slice(0, 4))
                link(nc.vector.memset(acc[:], 0.0))
                dve.wait_ge(rstd_done, norm + 1)

            nc.vector.memset(yh[:, 0].bitcast(F32), 0.0).then_inc(warm_ready, 1)
            link(nc.vector.memset(acc[:], 0.0))
            link(nc.vector.memset(axp[:, 0:A_CONV - 1], 0.0))

            for m in range(KT + LAG):
                if m < KT:
                    norm_lo(0, m)
                if m >= LAG:
                    norm_add(0, m - LAG, (m - LAG) % 2)
            lam = par[:, C_LRU:C_LRU + 8 * MT_A].rearrange("p (m k) -> p m k", k=8)[:, :, 7]
            dve.wait_ge(par_in, 16)
            link(ts(lru_rate, lam, -1.0, None, ALU.mult))
            tt(ln_var, lam, lru_rate, ALU.max).then_inc(lam_abs, 1)
            statistics(0)

            def decay_rate():
                dve.wait_ge(lam_exp, 1)
                link(ts(ln_var, ln_tmp, 2.0, None, ALU.add))
                link(nc.vector.reciprocal(ln_var, ln_var))
                link(tt(ln_tmp, ln_tmp, ln_var, ALU.mult))
                link(tt(ln_var, ln_tmp, ln_tmp, ALU.mult))
                link(ts(ln_rstd, ln_var, 1.0 / 17, None, ALU.mult))
                for k in range(15, 2, -2):
                    link(stt(ln_rstd, ln_rstd, 1.0 / k, ln_var, ALU.add, ALU.mult))
                link(stt(ln_rstd, ln_rstd, 1.0, ln_tmp, ALU.add, ALU.mult))
                link(ts(lru_rate, lru_rate, 0.0, None, ALU.max))
                link(stt(lru_rate, ln_rstd, 2.0, lru_rate, ALU.mult, ALU.add))
                ts(lru_rate, lru_rate, -8.0, None, ALU.mult).then_inc(rate_done, 1)

            def scaled_out(unit, dst):
                index = unit if unit < U_GATES else unit - 1 if unit <= U_AG0 else unit - 2
                dve.wait_ge(w_used, unit + 1)
                tt(dst, bank[MIX_BANKS[index % 4]][:], rstd[:], ALU.mult).then_inc(mix_free, 1)
                dve.wait_ge(mix_free, index + 1)

            def conv_lo(m):
                dve.wait_ge(ax_hi, m + 1)
                tt(mxl[:, m], axc[:, m], mxh[:, m], ALU.subtract).then_inc(ax_lo, 1)

            for m in range(MT_A):
                if m:
                    dve.wait_ge(ax_conv, m)
                scaled_out(U_AX + m, axp[:, A_CONV - 1:])
                link(ts(axc[:, m], axp[:, 3:3 + T], lru_par(m, 3), lru_par(m, 4), ALU.mult, ALU.add))
                link(stt(axc[:, m], axp[:, 2:2 + T], lru_par(m, 2), axc[:, m], ALU.mult, ALU.add))
                link(stt(axc[:, m], axp[:, 1:1 + T], lru_par(m, 1), axc[:, m], ALU.mult, ALU.add))
                stt(axc[:, m], axp[:, 0:T], lru_par(m, 0), axc[:, m], ALU.mult, ALU.add).then_inc(ax_conv, 1)
                if m:
                    conv_lo(m - 1)
                if m == 1:
                    dve.wait_ge(rel_in, 16)
                    link(ts(ext[:, 0:EXT_CLIP], relt[:, 0:1].to_broadcast([HEADS, EXT_CLIP]), -1.0, None, ALU.mult))
                    ts(ext[:, EXT_CLIP:EXT], relt[:, 0:EXT - EXT_CLIP], -1.0, None, ALU.mult).then_inc(ext_done, 1)
            conv_lo(MT_A - 1)
            for m in range(MT_A):
                scaled_out(U_BV + m, vg[:, m])
            decay_rate()
            for m in range(MT_A):
                dve.wait_ge(gate_sig, 2 * m + 2)
                tt(axc[:, m], axc[:, m], expm[:, m], ALU.mult).then_inc(ix_done, 1)
            for m in range(MT_A):
                dve.wait_ge(tanh_done, m + 1)
                link(tt(rec[:, m], decay[:, m], decay[:, m], ALU.mult))
                stt(expm[:, m], rec[:, m], 1.0, expm[:, m], ALU.add, ALU.mult).then_inc(expm_done, 1)
            for n in range(4):
                dve.wait_ge(tr_mm, n + 1)
                link(nc.vector.bn_stats(bn6[:, n], bank[SIDE_BANKS[n]][:]))
                link(nc.vector.bn_aggr(ln_mv[:, n], bn6[:, n]))
            ts(ln_var, ln_mv[:, :, 1], EPS, None, ALU.add).then_inc(ln_var_done, 1)
            dve.wait_ge(ln_root, 1)
            link(nc.vector.reciprocal(ln_rstd, ln_rstd))
            link(tt(ln_tmp, ln_rstd, ln_rstd, ALU.mult))
            link(tt(ln_tmp, ln_tmp, ln_var, ALU.mult))
            link(ts(ln_tmp, ln_tmp, -0.5, 1.5, ALU.mult, ALU.add))
            link(tt(ln_rstd, ln_rstd, ln_tmp, ALU.mult))
            dve.wait_ge(ln_in, 16 * 4)
            for n in range(4):
                stt(vg[:, n], bank[SIDE_BANKS[n]][:], ln_mv[:, n, 0:1], lng[:], ALU.subtract, ALU.mult).then_inc(ln_norm, 1)
                dve.wait_ge(ln_norm, n + 1)
                stt(vg[:, n], vg[:, n], ln_rstd[:, n:n + 1], lnb[:], ALU.mult, ALU.add).then_inc(ln_affine, 1)
                if n == 1:
                    scaled_out(U_BU, gu[:, 0])

            def recurrence(m):
                dve.wait_ge(expm_root, m + 1)
                link(tt(expm[:, m], expm[:, m], axc[:, m], ALU.mult))
                link(nc.vector.tensor_tensor_scan(rec[:, m], decay[:, m], expm[:, m], 0.0, ALU.mult, ALU.add))

            def v_split_lo(n):
                dve.wait_ge(v_hi, n + 1)
                tt(mxl[:, n], vg[:, n], mxh[:, n], ALU.subtract).then_inc(v_lo, 1)

            recurrence(0)
            v_split_lo(0)
            v_split_lo(1)
            v_split_lo(2)
            v_split_lo(3)
            scaled_out(U_BU + 1, gu[:, 1])
            scaled_out(U_BU + 2, gu[:, 2])

            def gated_product(m):
                dve.wait_ge(gelu_g, m + 1)
                tt(rec[:, m], rec[:, m], axp[:, 0:T], ALU.mult).then_inc(y_prod, 1)

            def y_split_lo(s):
                src = rec if Y_ORDER[s] < MT_A else vg
                dve.wait_ge(y_hi, s + 1)
                tt(yl[:, Y_ORDER[s]], src[:, Y_ORDER[s] % MT_A], yh[:, Y_ORDER[s]], ALU.subtract).then_inc(y_lo, 1)

            for gp in range(GROUPS // 2):
                for half in range(2):
                    item = 2 * gp + half
                    if item < GROUPS - 1:
                        dve.wait_ge(sgu_mm, item + 1)
                    else:
                        dve.wait_ge(w_used, U_SGU + 1)
                    ps = bank[SIDE_BANKS[item % 4]][:].rearrange("p (n g i) -> p n g i", n=2, g=2)
                    for g in range(2):
                        rows = slice(64 * g, 64 * g + 64)
                        ins = tt(vg[rows, gp, half * 256:half * 256 + 256].rearrange("p (n i) -> p n i", n=2),
                                 ps[rows, :, g, :], sgb[rows, gp:gp + 1, :].to_broadcast([64, 2, P]), ALU.add)
                        if g:
                            ins.then_inc(sgu_free, 1)
                        else:
                            ins.then_inc(dve_step, 1)
                            steps.n += 1
                dve.wait_ge(dve_step, steps.value())
                dve.wait_ge(sgu_free, 2 * gp + 2)
                dve.wait_ge(gelu_u, gp + 1)
                tt(vg[:, gp], vg[:, gp], gu[:, gp], ALU.mult).then_inc(y_prod, 1)
                if gp == 0:
                    scaled_out(U_BU + 3, gu[:, 3])
            scaled_out(U_AG0, axp[:, 0:T])
            for s in range(4):
                y_split_lo(s)
            gated_product(0)
            for m in range(1, MT_A):
                dve.wait_ge(y_prod, 4 + m)
                scaled_out(U_AG1 + m - 1, axp[:, 0:T])
                recurrence(m)
                y_split_lo(3 + m)
                gated_product(m)
            y_split_lo(3 + MT_A)

            def residual_tiles(first_unit, stage):
                for m in range(KT):
                    dve.wait_ge(w_used, first_unit + m + 1)
                    tt(x[:, m], x[:, m], bank[RES_BANKS[stage][m]][:], ALU.add).then_inc(x_ready, 1)
                    norm_tile(stage + 1, m, m % 2)
                statistics(stage + 1)

            def ffn(layer):
                base = U_UP[layer]
                for b in ub:
                    link(nc.vector.memset(b[:, 0:2], 0.0))

                def conv(t, turn, u, c, at):
                    dve.wait_ge(w_used, base + t + 1 + RAW * turn)
                    tt(u[:, 2:], bank[UP_BANKS[t % 6]][:], rstd[:], ALU.mult).then_inc(up_free[layer], 1)
                    dve.wait_ge(up_free[layer], t + 1 + RAW * turn)
                    tap = [par[:, bass.ds(at + k, 1)] if not isinstance(at, int) else par[:, at + k:at + k + 1]
                           for k in range(4)]
                    link(ts(c[:], u[:, 2:2 + T], tap[2], tap[3], ALU.mult, ALU.add))
                    link(stt(c[:], u[:, 1:1 + T], tap[1], c[:], ALU.mult, ALU.add))
                    stt(c[:], u[:, 0:T], tap[0], c[:], ALU.mult, ALU.add).then_inc(conv_done[layer], 1)

                cols = C_FFN + layer * FFN_COLS
                with dve.Fori(0, FF_PAIRS // 3) as turn:
                    steps.enter(turn, 12)
                    for j in range(3):
                        conv(2 * j, turn, ub[0], bank[CONV_BANKS[0]], cols + 8 * j + 24 * turn)
                        up = bank[CONV_BANKS[1]]
                        conv(2 * j + 1, turn, ub[1], up, cols + 8 * j + 4 + 24 * turn)
                        dve.wait_ge(silu_done[layer], j + 1 + 3 * turn)
                        dve.wait_ge(conv_done[layer], 2 * j + 2 + 6 * turn)
                        tt(up[:], cg[:], up[:], ALU.mult).then_inc(prod_done[layer], 1)
                        dve.wait_ge(act_hi[layer], j + 1 + 3 * turn)
                        pair = j + 3 * turn
                        tt(al[:, bass.ds(pair, 1), :], up[:].rearrange("p (a t) -> p a t", a=1),
                           ah[:, bass.ds(pair, 1), :], ALU.subtract).then_inc(act_lo[layer], 1)
                        dve.wait_ge(act_lo[layer], pair + 1)
                    steps.leave(FF_PAIRS // 3)
                conv(2 * FF_PAIRS, 0, ub[0], cg, cols + 8 * FF_PAIRS)
                dve.wait_ge(conv_done[layer], 2 * FF_PAIRS + 1)
                link(nc.vector.tensor_copy(cu[0:FF_TAIL], cg[FF_TAIL:P]))
                dve.wait_ge(silu_done[layer], FF_KT)
                tt(cu[0:FF_TAIL], cg[0:FF_TAIL], cu[0:FF_TAIL], ALU.mult).then_inc(prod_done[layer], 1)
                dve.wait_ge(act_hi[layer], FF_KT)
                tt(ah[FF_TAIL:P, FF_PAIRS], cu[0:FF_TAIL], ah[0:FF_TAIL, FF_PAIRS],
                   ALU.subtract).then_inc(act_lo[layer], 1)

                stage = 1 + 2 * layer
                base_d = U_DOWN[layer]

                def down(mm, turn):
                    m = mm + 2 * turn
                    dve.wait_ge(w_used, base_d + 3 * mm + 3 + RAW * turn)
                    xm = tile_of(x, m)
                    ps = bank[RES_BANKS[stage][mm]][:]
                    tt(xm, xm, ps if isinstance(m, int) else ps.rearrange("p (a t) -> p a t", a=1),
                       ALU.add).then_inc(x_ready, 1)
                    norm_tile(stage + 1, m, mm)

                with dve.Fori(0, KT // 2 - 1) as turn:
                    for mm in range(2):
                        down(mm, turn)
                down(0, KT // 2 - 1)
                if layer == 0:
                    down(1, KT // 2 - 1)
                    statistics(stage + 1)

            residual_tiles(U_OUT, 0)
            ffn(0)

            def qkv_evacuate(c, turn, which):
                dve.wait_ge(w_used, U_QKV + 3 * c + which + 1 + RAW * turn)
                ps = bank[proj_bank(c, turn, which)]
                if which < 2 and (c >= 1 or not isinstance(turn, int)):
                    dve.wait_ge(qk_lo, 2 * c + which - 1 + 4 * turn)
                if which == 0:
                    stt(q_sb[:], ps[:], -(HD ** -0.5), rstd[:], ALU.mult, ALU.mult).then_inc(qkv_out, 1)
                else:
                    tt((k_sb, v_sb)[which - 1][:], ps[:], rstd[:], ALU.mult).then_inc(qkv_out, 1)

            def qk_split_lo(c, turn, which):
                dve.wait_ge(qk_hi, 2 * c + which + 1 + 4 * turn)
                hi, lo = (kh, kl) if which else (qh, ql)
                tt(lo[:], (k_sb if which else q_sb)[:], hi[:], ALU.subtract).then_inc(qk_lo, 1)

            def scores(c, turn, g):
                if g == 0:
                    dve.wait_ge(bias_in[c % 2], 16 * (c // 2 + 1) + 16 * turn)
                    if c >= 1 or not isinstance(turn, int):
                        dve.wait_ge(ptr_mm, 7 * c + 14 * turn)
                for hh in range(2):
                    dve.wait_ge(score_mm, 6 * c + 2 * g + hh + 1 + 12 * turn)
                    nc.vector.memset(gate_word[:, 3 * hh + g:3 * hh + g + 1], 0.0)
                    for i, col in SCORE_GROUPS[g]:
                        n = P * (i + 1)
                        nc.vector.tensor_tensor_reduce(
                            out=p_sb[:, hh, P_OFF[i]:P_OFF[i] + n],
                            in0=bank[SCORE_BANKS[g][hh]][:, col:col + n], in1=bias[:, c % 2, hh, T - n:T],
                            scale=1.0, scalar=3.0e38, op0=ALU.add, op1=ALU.min,
                            accum_out=neg_min[:, 4 * hh + i:4 * hh + i + 1]).then_inc(score_out, 1)

            def normalise(c, turn, steps):
                for s in steps:
                    hh, i = SCORE_STEPS[s]
                    dve.wait_ge(exp_done, 8 * c + s + 1 + 16 * turn)
                    r = psums[:, 4 * hh + i:4 * hh + i + 1]
                    nc.vector.reciprocal(r, r).then_inc(rsum_inv, 1)
                    dve.wait_ge(rsum_inv, 8 * c + s + 1 + 16 * turn)
                    blk = p_sb[:, hh, P_OFF[i]:P_OFF[i] + P * (i + 1)]
                    ts(blk, blk, r, None, ALU.mult).then_inc(p_norm, 1)

            def transposed_split_lo(c, turn, t):
                dve.wait_ge(ptr_hi, 7 * c + t + 1 + 14 * turn)
                src = bank[TR_BANKS[(c + t) % 2]]
                if t == 0:
                    tt(vv[:, :, :, HD:P], src[:].rearrange("p (j h d) -> p j h d", j=4, h=2), vv[:, :, :, 0:HD],
                       ALU.subtract).then_inc(ptr_lo, 1)
                    return
                hh, g = (t - 1) // 3, (t - 1) % 3
                n = P * len(TR_GROUPS[g])
                tt(ptl[:, hh, TR_OFF[g]:TR_OFF[g] + n], src[:, 0:n], pth[:, hh, TR_OFF[g]:TR_OFF[g] + n],
                   ALU.subtract).then_inc(ptr_lo, 1)

            def o_add(c, turn, hh):
                dve.wait_ge(o_half, 2 * c + hh + 1 + 4 * turn)
                half = slice(HD * hh, HD * hh + HD)
                tt(o_sb[half], bank[AV_BANK][half, :], o_sb[half], ALU.add).then_inc(o_sum, 1)

            def o_split_lo(c, turn, hh):
                dve.wait_ge(o_hi, 2 * c + hh + 1 + 4 * turn)
                half = slice(HD * hh, HD * hh + HD)
                pair = c + 2 * turn
                src = o_sb[half, :]
                if isinstance(turn, int):
                    tt(ol[half, pair], src, oh[half, pair], ALU.subtract).then_inc(o_lo, 1)
                else:
                    tt(ol[half, bass.ds(pair, 1), :], src.rearrange("p (a t) -> p a t", a=1),
                       oh[half, bass.ds(pair, 1), :], ALU.subtract).then_inc(o_lo, 1)

            def attend(c, turn, following):
                transposed_split_lo(c, turn, 0)
                scores(c, turn, 0)
                scores(c, turn, 1)
                normalise(c, turn, range(2))
                scores(c, turn, 2)
                normalise(c, turn, range(2, 8))
                if following:
                    qkv_evacuate(c + 1, turn, 0)
                    qk_split_lo(c + 1, turn, 0)
                for t in (1, 2, 3):
                    transposed_split_lo(c, turn, t)
                if following:
                    qkv_evacuate(c + 1, turn, 1)
                    qk_split_lo(c + 1, turn, 1)
                transposed_split_lo(c, turn, 4)
                o_add(c, turn, 0)
                transposed_split_lo(c, turn, 5)
                o_split_lo(c, turn, 0)
                transposed_split_lo(c, turn, 6)
                if following:
                    qkv_evacuate(c + 1, turn, 2)
                o_add(c, turn, 1)
                o_split_lo(c, turn, 1)

            qkv_evacuate(0, 0, 0)
            qkv_evacuate(0, 0, 1)
            qk_split_lo(0, 0, 0)
            qk_split_lo(0, 0, 1)
            qkv_evacuate(0, 0, 2)
            attend(0, 0, True)
            attend(1, 0, True)
            with dve.Fori(0, PAIRS // 2 - 2) as turn:
                attend(2, turn, True)
                attend(3, turn, True)
            attend(PAIRS - 2, 0, True)
            attend(PAIRS - 1, 0, False)
            residual_tiles(U_WO, 2)
            ffn(1)

            for half in range(2):
                cols, col2 = slice(HALF * half, HALF * half + HALF), slice(2 * half, 2 * half + 2)
                last = x[:, KT - 1, cols]
                dve.wait_ge(final_mm, half + 1)
                tt(last, last, bank[FINAL_BANKS[half]][:, 0:HALF], ALU.add).then_inc(x_last, 1)
                dve.wait_ge(root_done, 5 + half)
                inverse_root(bank[FINAL_STAT_BANKS[half]][:, 0:2], col2)
                dve.wait_ge(x_hi, 5 * KT - 1)
                dve.wait_ge(x_last, half + 1)
                dve.wait_ge(rstd_done, 5 + half)
                for m in range(OUT_POOL, KT - 1):
                    tt(x[:, m, cols], x[:, m, cols], rstd[:, cols], ALU.mult).then_inc(out_dve, 1)
                stt(last, last, gain(4, KT - 1), rstd[:, cols], ALU.mult, ALU.mult).then_inc(out_dve, 1)

        @block.tensor
        def _(pe):
            def product(dst, w_hi_part, w_lo_part, m_hi, m_lo, first, last):
                nc.tensor.matmul(dst, w_hi_part, m_hi, start=first, stop=False)
                nc.tensor.matmul(dst, w_hi_part, m_lo, start=False, stop=False)
                return nc.tensor.matmul(dst, w_lo_part, m_hi, start=False, stop=last)

            def tiles(dst, unit, ks, first, last, src=(None, None)):
                mh, ml = src
                slot = unit % RING
                for n, k in enumerate(ks):
                    ins = product(dst, wh[:, slot, k], wl[:, slot, k], mh[:, k], ml[:, k],
                                  first and n == 0, last and n == len(ks) - 1)
                return ins

            def whole(unit, b, turn=0, src=None):
                pe.wait_ge(w_lo, unit + 1 + RAW * turn)
                tiles(bank[b][:], unit, range(KT), True, True, src or (xh, xl)).then_inc(w_used, 1)

            def first_units(unit, banks, norm):
                a, b = bank[banks[0]][:], bank[banks[1]][:]
                src = (xh, xl)
                pe.wait_ge(w_lo, unit + 1)
                for k in range(KT - 1):
                    pe.wait_ge(x_lo, norm * KT + k + 1)
                    tiles(a, unit, [k], k == 0, False, src)
                pe.wait_ge(w_lo, unit + 2)
                tiles(b, unit + 1, range(4), True, False, src)
                statistics(norm)
                tiles(b, unit + 1, range(4, KT - 1), False, False, src)
                pe.wait_ge(x_lo, (norm + 1) * KT)
                tiles(a, unit, [KT - 1], False, True, src).then_inc(w_used, 1)
                spread_rstd(norm)
                tiles(b, unit + 1, [KT - 1], False, True, src).then_inc(w_used, 1)

            def statistics(norm):
                pe.wait_ge(x_acc, norm * KT + KT)
                for j in range(4):
                    ins = nc.tensor.matmul(bank[STAT_BANK][:, j:j + 1], acc[:, P * j:P * j + P], mean_w,
                                           start=True, stop=True)
                ins.then_inc(stat_mm, 1)

            def spread_rstd(norm):
                pe.wait_ge(col_done, norm + 1)
                for j in range(4):
                    ins = nc.tensor.matmul(bank[STAT_BANK][:, P * j:P * j + P],
                                           rstd_col[:, j:j + 1].to_broadcast([P, P]), ident[:], start=True, stop=True)
                ins.then_inc(spread_mm, 1)

            pe.wait_ge(warm_ready, 1)
            for _ in range(WARM_UP):
                nc.tensor.matmul(bank[STAT_BANK][:], yh[:, 0, 0:P], yh[:, 0], start=True, stop=True)
            pe.wait_ge(const_done, 3)
            pe.wait_ge(ident_done, 1)
            pe.wait_ge(first_lo, 1)
            for k in range(KT):
                if k == FIRST // P:
                    pe.wait_ge(w_lo, 1)
                pe.wait_ge(x_lo, k + 1)
                ins = tiles(bank[MIX_BANKS[0]][:], U_AX, [k], k == 0, k == KT - 1, (xh, xl))
            ins.then_inc(w_used, 1)
            whole(U_AX + 1, MIX_BANKS[1])
            statistics(0)
            pe.wait_ge(w_lo, U_AX + 3)
            tiles(bank[MIX_BANKS[2]][:], U_AX + 2, range(3), True, False, (xh, xl))
            spread_rstd(0)
            tiles(bank[MIX_BANKS[2]][:], U_AX + 2, range(3, KT), False, True, (xh, xl)).then_inc(w_used, 1)
            for c in range(3, U_GATES):
                if c >= 4:
                    pe.wait_ge(mix_free, c - 3)
                whole(c, MIX_BANKS[c % 4])
            slot = U_GATES % RING
            pe.wait_ge(w_lo, U_GATES + 1)
            for item in range(2 * MT_A):
                m, g = item // 2, item % 2
                if item == MT_A:
                    pe.wait_ge(mix_free, U_BU - 1 - 3)
                    pe.wait_ge(w_lo, U_BU + 1)
                    tiles(bank[MIX_BANKS[0]][:], U_BU, range(3), True, False, (xh, xl))
                if g == 0:
                    pe.wait_ge(ax_lo, m + 1)
                if item == 1:
                    pe.wait_ge(rstd_done, 1)
                if item >= 4:
                    pe.wait_ge(gate_sig, item - 3)
                k = g * MT_A + m
                ins = product(bank[SIDE_BANKS[item % 4]][:], wh[:, slot, k], wl[:, slot, k],
                              mxh[:, m], mxl[:, m], True, True)
                ins.then_inc(w_used if item == 2 * MT_A - 1 else gates_mm, 1)
            pe.wait_ge(gelu_v, MT_A)
            for n in range(4):
                pe.wait_ge(gate_sig, 5 + n)
                for m in range(MT_A):
                    ins = nc.tensor.transpose(bank[SIDE_BANKS[n]][:, P * m:P * m + P], vg[:, m, P * n:P * n + P],
                                              ident[:])
                ins.then_inc(tr_mm, 1)
            tiles(bank[MIX_BANKS[0]][:], U_BU, range(3, KT), False, True, (xh, xl)).then_inc(w_used, 1)
            for c in range(U_BU + 1, U_AG0 + 1):
                pe.wait_ge(mix_free, c - 1 - 3)
                whole(c, MIX_BANKS[(c - 1) % 4])
            slot = U_SGU % RING
            pe.wait_ge(w_lo, U_SGU + 1)
            for item in range(GROUPS):
                gp, half = item // 2, item % 2
                if item == 4:
                    pe.wait_ge(mix_free, U_AG1 - 2 - 3)
                    pe.wait_ge(w_lo, U_AG1 + 1)
                    tiles(bank[MIX_BANKS[(U_AG1 - 2) % 4]][:], U_AG1, range(4), True, False, (xh, xl))
                if item < 2:
                    pe.wait_ge(v_lo, 2 * half + 2)
                if item < 4:
                    pe.wait_ge(ln_norm, item + 1)
                else:
                    pe.wait_ge(sgu_free, item - 3)
                for n in range(2):
                    ins = product(bank[SIDE_BANKS[item % 4]][:, 256 * n:256 * n + 256],
                                  mxh[:, 2 * half + n, P * gp:P * gp + P], mxl[:, 2 * half + n, P * gp:P * gp + P],
                                  wh[:, slot, 2 * gp:2 * gp + 2].rearrange("p a b -> p (a b)"),
                                  wl[:, slot, 2 * gp:2 * gp + 2].rearrange("p a b -> p (a b)"), True, True)
                ins.then_inc(w_used if item == GROUPS - 1 else sgu_mm, 1)
            tiles(bank[MIX_BANKS[(U_AG1 - 2) % 4]][:], U_AG1, range(4, KT), False, True, (xh, xl)).then_inc(w_used, 1)
            for c in range(U_AG1 + 1, U_OUT):
                pe.wait_ge(mix_free, c - 2 - 3)
                whole(c, MIX_BANKS[(c - 2) % 4])

            def residual_start(unit, banks, src, order, ready):
                for b in range(2):
                    pe.wait_ge(w_lo, unit + b + 1)
                    for n, k in enumerate(order[:-1]):
                        ready(n)
                        tiles(bank[banks[b]][:], unit + b, [k], n == 0, False, src)
                ready(KT - 1)
                for b in range(2):
                    tiles(bank[banks[b]][:], unit + b, [order[-1]], False, True, src).then_inc(w_used, 1)

            def residual_rest(unit, stage, src, first):
                for m in range(first, KT):
                    if RES_BANKS[stage][m] == RES_BANKS[stage][m - 2]:
                        pe.wait_ge(x_ready, stage * KT + m - 1)
                    whole(unit + m, RES_BANKS[stage][m], src=src)

            pe.wait_ge(sgu_free, GROUPS)
            residual_start(U_OUT, RES_BANKS[0], (yh, yl), Y_ORDER, lambda n: pe.wait_ge(y_lo, n + 1))
            residual_rest(U_OUT, 0, (yh, yl), 2)

            def ffn(layer):
                base = U_UP[layer]
                first_units(base, UP_BANKS, 1 + 2 * layer)
                for t in range(2, 6):
                    if t == 5:
                        pe.wait_ge(rstd_done, 2 + 2 * layer)
                    whole(base + t, UP_BANKS[t])
                with pe.Fori(0, FF_PAIRS // 3 - 1) as turn:
                    for t in range(6):
                        pe.wait_ge(up_free[layer], t + 1 + 6 * turn)
                        whole(base + 6 + t, UP_BANKS[t], turn)
                pe.wait_ge(up_free[layer], 2 * FF_PAIRS - 5)
                whole(base + 2 * FF_PAIRS, UP_BANKS[0])

                stage = 1 + 2 * layer
                base = U_DOWN[layer]

                def k_tile(dst, m, kt, cols, turn=0):
                    u, k = divmod(kt, KT)
                    slot = (base + 3 * m + u) % RING
                    if k == 0:
                        pe.wait_ge(w_lo, base + 3 * m + u + 1 + RAW * turn)
                    if m == 0:
                        pe.wait_ge(act_lo[layer], kt + 1)
                    if kt < FF_PAIRS:
                        return product(dst, wh[:, slot, k], wl[:, slot, k], ah[:, kt, cols], al[:, kt, cols],
                                       kt == 0, False)
                    nc.tensor.matmul(dst, wh[:, slot, k], ah[:, kt, cols], start=False, stop=False)
                    return nc.tensor.matmul(dst, wl[0:FF_TAIL, slot, k], ah[0:FF_TAIL, kt, cols],
                                            start=False, stop=True)

                def down(mm, turn):
                    pe.wait_ge(x_ready, stage * KT + mm - 1 + 2 * turn)
                    for kt in range(FF_KT):
                        ins = k_tile(bank[RES_BANKS[stage][mm]][:], mm, kt, slice(0, T), turn)
                        if kt % KT == KT - 1 or kt == FF_KT - 1:
                            ins.then_inc(w_used, 1)

                assert RES_BANKS[stage][0] == CONV_BANKS[0]
                pe.wait_ge(silu_done[layer], FF_PAIRS)
                with pe.Fori(0, KT // 2 - layer) as turn:
                    for mm in range(2):
                        down(mm, turn)
                if layer:
                    down(0, KT // 2 - 1)
                    pe.wait_ge(x_ready, stage * KT + KT - 2)
                    for half in range(2):
                        for kt in range(FF_KT):
                            if half and kt == 5:
                                final_statistics(0)
                            if half and kt == 12:
                                final_spread(0)
                            ins = k_tile(bank[FINAL_BANKS[half]][:, 0:HALF], KT - 1, kt,
                                         slice(HALF * half, HALF * half + HALF))
                        ins.then_inc(final_mm, 1)
                    final_statistics(1)
                    final_spread(1)

            def final_statistics(half):
                stat = bank[FINAL_STAT_BANKS[half]]
                pe.wait_ge(x_acc, 5 * KT - 1)
                pe.wait_ge(final_sq, half + 1)
                for j in range(2):
                    at = HALF * half + P * j
                    nc.tensor.matmul(stat[:, j:j + 1], acc[:, at:at + P], mean_w, start=True, stop=False)
                    ins = nc.tensor.matmul(stat[:, j:j + 1], sq[:, 1, at:at + P], mean_w, start=False, stop=True)
                ins.then_inc(stat_mm, 1)

            def final_spread(half):
                pe.wait_ge(col_done, 5 + half)
                for j in range(2):
                    r = rstd_col[:, 2 * half + j:2 * half + j + 1]
                    ins = nc.tensor.matmul(bank[FINAL_STAT_BANKS[half]][:, P * j:P * j + P],
                                           r.to_broadcast([P, P]), ident[:], start=True, stop=True)
                ins.then_inc(spread_mm, 1)

            ffn(0)

            def transpose_v(c, turn):
                if c >= 1 or not isinstance(turn, int):
                    pe.wait_ge(ptr_lo, 7 * c - 1 + 14 * turn)
                pe.wait_ge(qkv_out, 3 * c + 3 + 6 * turn)
                for n in range(4):
                    ins = nc.tensor.transpose(bank[TR_BANKS[c % 2]][:, P * n:P * n + P], v_sb[:, P * n:P * n + P],
                                              ident[:])
                ins.then_inc(ptr_mm, 1)

            def scores(c, turn, g):
                if g == 0:
                    pe.wait_ge(qk_lo, 2 * c + 2 + 4 * turn)
                    if c >= 1 or not isinstance(turn, int):
                        pe.wait_ge(score_out, 8 * c + 16 * turn)
                elif g == 1:
                    if c >= 1 or not isinstance(turn, int):
                        pe.wait_ge(o_sum, 2 * c + 4 * turn)
                else:
                    pe.wait_ge(score_out, 8 * c + 2 + 16 * turn)
                for n, (i, col) in enumerate(SCORE_GROUPS[g]):
                    keys = P * (i + 1)
                    for q, k, start, stop in ((qh, kh, True, False), (qh, kl, False, False), (ql, kh, False, True)):
                        for hh in range(2):
                            rows = slice(HD * hh, HD * hh + HD)
                            ins = nc.tensor.matmul(bank[SCORE_BANKS[g][hh]][:, col:col + keys],
                                                   q[rows, P * i:P * i + P], k[rows, 0:keys],
                                                   start=start, stop=stop)
                            if stop and n == len(SCORE_GROUPS[g]) - 1:
                                ins.then_inc(score_mm, 1)

            def transpose_p(c, turn, t):
                hh, g = (t - 1) // 3, (t - 1) % 3
                if t == 1:
                    pe.wait_ge(p_norm, 8 * c + 7 + 16 * turn)
                elif t == 4:
                    pe.wait_ge(p_norm, 8 * c + 8 + 16 * turn)
                if t >= 2 or c >= 1 or not isinstance(turn, int):
                    pe.wait_ge(ptr_lo, 7 * c + t - 1 + 14 * turn)
                for n, (i, j) in enumerate(TR_GROUPS[g]):
                    ins = nc.tensor.transpose(bank[TR_BANKS[(c + t) % 2]][:, P * n:P * n + P],
                                              p_sb[:, hh, P_OFF[i] + P * j:P_OFF[i] + P * j + P], ident[:])
                ins.then_inc(ptr_mm, 1)

            def weighted_v(c, turn, hh):
                pe.wait_ge(ptr_lo, 7 * c + 3 * hh + 4 + 14 * turn)
                if hh:
                    pe.wait_ge(o_sum, 2 * c + 1 + 4 * turn)
                else:
                    pe.wait_ge(score_out, 8 * c + 6 + 16 * turn)
                for j in range(4):
                    src = slice(KEY_OFF[j], KEY_OFF[j] + T - P * j)
                    nc.tensor.matmul(bank[AV_BANK][:, P * j:T], vv[:, j, hh], pth[:, hh, src],
                                     start=j == 0, stop=False)
                    ins = nc.tensor.matmul(bank[AV_BANK][:, P * j:T], vv[:, j, hh], ptl[:, hh, src],
                                           start=False, stop=j == 3)
                ins.then_inc(av_mm, 1)

            def project(c, turn, which, ks=range(KT)):
                unit = U_QKV + 3 * c + which
                first, last = ks[0] == 0, ks[-1] == KT - 1
                if first:
                    pe.wait_ge(w_lo, unit + 1 + RAW * turn)
                    if c >= 1 or not isinstance(turn, int):
                        pe.wait_ge(qkv_out, 3 * c + which - 1 + 6 * turn)
                dst = bank[proj_bank(c, turn, which)][:]
                ins = tiles(dst, unit, ks, first, last, (xh, xl))
                if last:
                    ins.then_inc(w_used, 1)

            def attend(c, turn, fill):
                if c or not isinstance(turn, int):
                    transpose_v(c, turn)
                    scores(c, turn, 0)
                else:
                    scores(c, turn, 0)
                    transpose_v(c, turn)
                fill(0)
                scores(c, turn, 1)
                fill(1)
                scores(c, turn, 2)
                fill(2)
                transpose_p(c, turn, 1)
                transpose_p(c, turn, 2)
                fill(3)
                transpose_p(c, turn, 3)
                fill(4)
                transpose_p(c, turn, 4)
                fill(5)
                weighted_v(c, turn, 0)
                transpose_p(c, turn, 5)
                fill(6)
                transpose_p(c, turn, 6)
                fill(7)
                weighted_v(c, turn, 1)

            def next_pair(c, turn):
                parts = [[(0, 0, 2)], [(0, 2, 5)], [(0, 5, KT), (1, 0, 4)], [(1, 4, 6)], [(1, 6, KT)], [(2, 0, 2)],
                         [(2, 2, 4)], [(2, 4, KT)]]

                def fill(n):
                    for which, k0, k1 in parts[n]:
                        project(c + 1, turn, which, range(k0, k1))
                return fill

            first_units(U_QKV, ATT_PROJ_BANKS, 2)
            project(0, 0, 2)
            attend(0, 0, next_pair(0, 0))
            attend(1, 0, next_pair(1, 0))
            with pe.Fori(0, PAIRS // 2 - 2) as turn:
                attend(2, turn, next_pair(2, turn))
                attend(3, turn, next_pair(3, turn))
            attend(PAIRS - 2, 0, next_pair(PAIRS - 2, 0))

            def output_part(n):
                for b, ks in ([(0, (0,))], [(0, (1, 2, 3))], [(0, (4, 5, 6)), (1, (0, 1, 2))], [(1, (3, 4))],
                              [(1, (5, 6))], [(2, (0,))], [(2, (1,))], [(2, (2, 3))], [(2, (4, 5, 6))])[n]:
                    if ks[0] == 0:
                        pe.wait_ge(w_lo, U_WO + b + 1)
                        pe.wait_ge(qkv_out, 3 * PAIRS)
                        if b == 2:
                            pe.wait_ge(score_out, 8 * PAIRS)
                    if b == 0:
                        pe.wait_ge(o_lo, 2 * ks[-1] + 2)
                    tiles(bank[RES_BANKS[2][b]][:], U_WO + b, ks, ks[0] == 0, False, (oh, ol))

            attend(PAIRS - 1, 0, output_part)
            output_part(8)
            pe.wait_ge(o_lo, HEADS)
            for b in range(3):
                tiles(bank[RES_BANKS[2][b]][:], U_WO + b, [KT - 1], False, True, (oh, ol)).then_inc(w_used, 1)
            residual_rest(U_WO, 2, (oh, ol), 3)
            ffn(1)



def column_tiles(w):
    return w.reshape(KT, P, -1, P).transpose(2, 1, 0, 3)


def pack_weights(w_in, gate_r, gate_i, sgu_w, w_out, w_qkv, w_o, w_up, w_down):
    zin = column_tiles(w_in)
    a_x, a_g, b_u, b_v = (zin[MT_A * q:MT_A * q + MT_A] for q in range(4))
    gates = np.zeros((1, P, KT, P), w_in.dtype)
    for g, w in enumerate((gate_r, gate_i)):
        for m in range(MT_A):
            for half in range(2):
                at = slice(64 * half, 64 * half + 64)
                gates[0, at, g * MT_A + m, at] = w[2 * m + half]
    sgu = sgu_w.transpose(2, 0, 1)[None]
    parts = [a_x, b_v, gates, b_u, a_g[0:1], sgu, a_g[1:], column_tiles(w_out)]

    def up(w):
        g = column_tiles(w[:, 0:FF_PAIRS * P])
        u = column_tiles(w[:, D_FF:D_FF + FF_PAIRS * P])
        pairs = np.stack([g, u], 1).reshape(2 * FF_PAIRS, P, KT, P)
        tail = np.concatenate([w[:, FF_PAIRS * P:D_FF], w[:, D_FF + FF_PAIRS * P:]], 1)
        return [pairs, column_tiles(tail)]

    def down(w):
        full = np.concatenate([w, w[FF_PAIRS * P:], np.zeros((3 * D - FF_KT * P, D), w.dtype)], 0)
        return full.reshape(3, KT, P, KT, P).transpose(3, 0, 2, 1, 4).reshape(3 * KT, P, KT, P)

    parts += up(w_up[0]) + [down(w_down[0])]
    parts.append(column_tiles(w_qkv).reshape(3, PAIRS, P, KT, P).transpose(1, 0, 2, 3, 4).reshape(-1, P, KT, P))
    parts.append(column_tiles(w_o))
    parts += up(w_up[1]) + [down(w_down[1])]
    return np.concatenate([p.reshape(-1, P, UNIT) for p in parts], 0)


def pack_params(norms, conv_w, conv_b, lru_conv_w, lru_conv_b, r_b, i_b, lam):
    cols = [n.reshape(KT, P).T for n in norms]
    for layer in range(2):
        rows = np.concatenate([conv_w[layer], conv_b[layer][None]], 0)
        g, u = rows[:, 0:D_FF], rows[:, D_FF:]
        full = np.stack([v[:, 0:FF_PAIRS * P].reshape(4, FF_PAIRS, P) for v in (g, u)])
        cols.append(full.transpose(3, 2, 0, 1).reshape(P, 8 * FF_PAIRS))
        tail = np.concatenate([g[:, FF_PAIRS * P:], u[:, FF_PAIRS * P:]], 1).T
        cols += [tail, np.zeros((P, 4), tail.dtype)]
    lru = np.concatenate([lru_conv_w, lru_conv_b[None], r_b[None], i_b[None], lam[None]], 0)
    cols.append(lru.reshape(8, MT_A, P).transpose(2, 1, 0).reshape(P, 8 * MT_A))
    return np.concatenate(cols, 1)


def kernel(**inputs):
    import concourse.bacc as bacc
    from concourse.bass_utils import run_bass_kernel_spmd

    a = {k: np.asarray(v) for k, v in inputs.items()}
    arrays = {
        "x_in": a["x"][0].T.reshape(KT, P, T).transpose(1, 0, 2),
        "weights": pack_weights(a["w_in_ab"][0], a["lru_gate_r_w"][0], a["lru_gate_i_w"][0], a["sgu_w"][0],
                                a["w_out_ab"][0], a["w_qkv"][0], a["w_o"][0], a["ffn_w_up"], a["ffn_w_down"]),
        "params": pack_params([a["norm_ab"][0], a["norm_ffn"][0], a["norm_attn"][0], a["norm_ffn"][1],
                               a["norm_final"]], a["ffn_conv_w"], a["ffn_conv_b"], a["lru_conv_w"][0],
                              a["lru_conv_b"][0], a["lru_gate_r_b"][0], a["lru_gate_i_b"][0], a["lru_lambda"][0]),
        "rel_rev": a["rel_bias"][0][:, ::-1],
        "ln_g": a["sgu_ln_g"],
        "ln_b": a["sgu_ln_b"],
        "sgu_b": a["sgu_b"][0],
    }
    arrays = {k: np.ascontiguousarray(v) for k, v in arrays.items()}
    nc = bacc.Bacc("TRN2", target_bir_lowering=False, num_devices=1)
    args = [nc.dram_tensor(n, v.shape, mybir.dt.from_np(v.dtype), kind="ExternalInput").ap()
            for n, v in arrays.items()]
    out = nc.dram_tensor("out", (P, KT, T), F32, kind="ExternalOutput").ap()
    trunk(nc, *args, out)
    got = run_bass_kernel_spmd(nc, [arrays], core_ids=[0]).results[0]["out"]
    return got.transpose(1, 0, 2).reshape(D, T).T[None]
```
